# Optimizing a Trainium2 kernel written in Bass

```python
import jax, jax.numpy as jnp
from jax import lax
import numpy as np

D_MODEL = 1024
BATCH = 1
SEQ = 512
DEPTH = 1

ATT_HEADS = 8
ATT_HD = 64
ATT_W = ATT_HEADS * ATT_HD
IDX_HEADS = 4
IDX_HD = 64
TOPK_MAX = 256
QBLOCK = 128
GLA_HEADS = 4
GLA_DK = 64
GLA_DV = 128
GLA_W = GLA_HEADS * GLA_DV
GLA_GATE_RANK = 16
GLA_TAU = 16.0
GLA_CHUNK = 64
ROPE_THETA = 500000.0
ROT_DIM = ATT_HD // 4
NORM_EPS = 1e-6
NEG = -1e30

PROJ_SIZES = (
    ATT_W, ATT_W, ATT_W,
    IDX_HEADS * IDX_HD,
    IDX_HD,
    IDX_HEADS,
    ATT_W,
    GLA_HEADS * GLA_DK,
    GLA_HEADS * GLA_DK,
    GLA_W,
    GLA_GATE_RANK,
    GLA_W,
)
PROJ_TOTAL = sum(PROJ_SIZES)

kernel_name = "hymba_dsa_gla_sandwich_block"

def _rmsnorm(x, w):
    xf = x.astype(jnp.float32)
    y = xf * lax.rsqrt(jnp.mean(xf * xf, axis=-1, keepdims=True) + NORM_EPS)
    return (y * w.astype(jnp.float32)).astype(x.dtype)

def _rope_tables(positions):
    inv = ROPE_THETA ** (-jnp.arange(0, ROT_DIM, 2, dtype=jnp.float32) / ROT_DIM)
    ang = positions.astype(jnp.float32)[..., None] * inv
    return jnp.cos(ang)[:, :, None, :], jnp.sin(ang)[:, :, None, :]

def _partial_rope(x, cos, sin):
    half = ROT_DIM // 2
    xf = x.astype(jnp.float32)
    x1 = xf[..., :half]
    x2 = xf[..., half:ROT_DIM]
    out = jnp.concatenate([x1 * cos - x2 * sin, x2 * cos + x1 * sin, xf[..., ROT_DIM:]], axis=-1)
    return out.astype(x.dtype)

def _dsa_attention(q, k, v, q_idx, k_idx, w_idx):
    B, S, H, dh = q.shape
    nb = S // QBLOCK
    ksel = min(TOPK_MAX, S // 4)
    key_pos = jnp.arange(S)
    k_idx_f = k_idx.astype(jnp.float32)
    gather = jax.vmap(lambda tab, ix: tab[ix])

    def to_blocks(a):
        return jnp.moveaxis(a.reshape((B, nb, QBLOCK) + a.shape[2:]), 1, 0)

    def block(args):
        qb, qib, wb, bi = args
        qpos = bi * QBLOCK + jnp.arange(QBLOCK)
        causal = key_pos[None, :] <= qpos[:, None]
        rel = jax.nn.relu(jnp.einsum('bqhd,bsd->bqhs', qib.astype(jnp.float32), k_idx_f))
        score = jnp.einsum('bqh,bqhs->bqs', wb.astype(jnp.float32), rel)
        score = jnp.where(causal[None], score, NEG)
        _, idx = lax.top_k(score, ksel)
        valid = idx <= qpos[None, :, None]
        kg = gather(k, idx)
        vg = gather(v, idx)
        logits = jnp.einsum('bqhd,bqkhd->bqhk', qb, kg).astype(jnp.float32) * (dh ** -0.5)
        logits = jnp.where(valid[:, :, None, :], logits, NEG)
        p = jax.nn.softmax(logits, axis=-1).astype(v.dtype)
        return jnp.einsum('bqhk,bqkhd->bqhd', p, vg)

    out = lax.map(block, (to_blocks(q), to_blocks(q_idx), to_blocks(w_idx), jnp.arange(nb)))
    return jnp.moveaxis(out, 0, 1).reshape(B, S, H, dh)

def _gla(q, k, v, g):
    B, S, H, dk = q.shape
    C = GLA_CHUNK
    nc = S // C

    def chunks(a):
        return jnp.transpose(a.reshape(B, nc, C, H, a.shape[-1]), (1, 0, 3, 2, 4))

    qc = chunks(q.astype(jnp.float32) * (dk ** -0.5))
    kc = chunks(k.astype(jnp.float32))
    vc = chunks(v.astype(jnp.float32))
    gc = chunks(g)
    tri = jnp.tril(jnp.ones((C, C), dtype=bool))

    def step(state, inp):
        qi, ki, vi, gi = inp
        b = jnp.cumsum(gi, axis=2)
        o_inter = jnp.einsum('bhtd,bhde->bhte', qi * jnp.exp(b), state)
        diff = b[:, :, :, None, :] - b[:, :, None, :, :]
        decay = jnp.exp(jnp.where(tri[None, None, :, :, None], diff, NEG))
        a = jnp.einsum('bhtd,bhsd,bhtsd->bhts', qi, ki, decay)
        o = o_inter + jnp.einsum('bhts,bhse->bhte', a, vi)
        b_last = b[:, :, -1:, :]
        new_state = (jnp.exp(b_last[:, :, 0, :])[..., None] * state
                     + jnp.einsum('bhsd,bhse->bhde', ki * jnp.exp(b_last - b), vi))
        return new_state, o

    state0 = jnp.zeros((B, H, dk, v.shape[-1]), jnp.float32)
    _, o = lax.scan(step, state0, (qc, kc, vc, gc))
    return jnp.transpose(o, (1, 0, 3, 2, 4)).reshape(B, S, H, v.shape[-1])

def setup_inputs(seed: int = 0) -> dict:
    key = jax.random.key(seed)
    ks = jax.random.split(key, 9)
    x = jax.random.normal(ks[0], (BATCH, SEQ, D_MODEL), jnp.float32)
    positions = jnp.broadcast_to(jnp.arange(SEQ, dtype=jnp.int32)[None, :], (BATCH, SEQ))
    w_in = jax.random.normal(ks[1], (D_MODEL, PROJ_TOTAL), jnp.float32) * D_MODEL ** -0.5
    w_gla_gate_up = jax.random.normal(ks[2], (GLA_GATE_RANK, GLA_HEADS * GLA_DK), jnp.float32) * GLA_GATE_RANK ** -0.5
    b_gla_gate = 0.01 * jax.random.normal(ks[3], (GLA_HEADS * GLA_DK,), jnp.float32)
    gla_norm_w = 1.0 + 0.02 * jax.random.normal(ks[4], (GLA_DV,), jnp.float32)
    w_out = jax.random.normal(ks[5], (ATT_W + GLA_W, D_MODEL), jnp.float32) * (ATT_W + GLA_W) ** -0.5
    pre_norm_w = 1.0 + 0.02 * jax.random.normal(ks[6], (D_MODEL,), jnp.float32)
    post_norm_w = 1.0 + 0.02 * jax.random.normal(ks[7], (D_MODEL,), jnp.float32)
    return {"x": x, "positions": positions, "w_in": w_in, "w_gla_gate_up": w_gla_gate_up,
            "b_gla_gate": b_gla_gate, "gla_norm_w": gla_norm_w, "w_out": w_out,
            "pre_norm_w": pre_norm_w, "post_norm_w": post_norm_w}

def reference(x, positions, w_in, w_gla_gate_up, b_gla_gate, gla_norm_w, w_out, pre_norm_w, post_norm_w):
    B, S, _ = x.shape
    cos, sin = _rope_tables(positions)
    for _layer in range(DEPTH):
        h = _rmsnorm(x, pre_norm_w)
        proj = h @ w_in
        splits = []
        acc = 0
        for sz in PROJ_SIZES[:-1]:
            acc += sz
            splits.append(acc)
        (a_q, a_k, a_v, i_q, i_k, i_w, a_gate,
         g_q, g_k, g_v, g_lr, g_gate) = jnp.split(proj, splits, axis=-1)

        a_q = _partial_rope(a_q.reshape(B, S, ATT_HEADS, ATT_HD), cos, sin)
        a_k = _partial_rope(a_k.reshape(B, S, ATT_HEADS, ATT_HD), cos, sin)
        a_v = a_v.reshape(B, S, ATT_HEADS, ATT_HD)
        i_q = _partial_rope(i_q.reshape(B, S, IDX_HEADS, IDX_HD), cos, sin)
        i_k = _partial_rope(i_k.reshape(B, S, 1, IDX_HD), cos, sin)[:, :, 0, :]
        i_w = i_w * (IDX_HEADS ** -0.5 * IDX_HD ** -0.5)
        att = _dsa_attention(a_q, a_k, a_v, i_q, i_k, i_w).reshape(B, S, ATT_W)
        att = att * jax.nn.silu(a_gate)

        log_alpha = jax.nn.log_sigmoid((g_lr @ w_gla_gate_up + b_gla_gate).astype(jnp.float32)) / GLA_TAU
        o = _gla(g_q.reshape(B, S, GLA_HEADS, GLA_DK), g_k.reshape(B, S, GLA_HEADS, GLA_DK),
                 g_v.reshape(B, S, GLA_HEADS, GLA_DV), log_alpha.reshape(B, S, GLA_HEADS, GLA_DK))
        o = _rmsnorm(o, gla_norm_w).astype(x.dtype).reshape(B, S, GLA_W)
        gla = o * jax.nn.silu(g_gate)

        mixed = jnp.concatenate([att, gla], axis=-1) @ w_out
        x = x + _rmsnorm(mixed, post_norm_w)
    return x


_drawn_inputs = setup_inputs


def setup_inputs(seed=0):
    import zlib

    import numpy as np

    out = dict(_drawn_inputs(seed))
    spreads = {}
    factors = {'b_gla_gate': 8.0, 'gla_norm_w': 4.109, 'post_norm_w': 4.057}
    for name, (base, spread) in spreads.items():
        noise = np.random.default_rng([zlib.crc32(name.encode()), seed]).standard_normal(out[name].shape)
        drawn = base * np.exp(spread * noise) if base else spread * noise
        out[name] = __import__('jax').numpy.asarray(drawn.astype(out[name].dtype))
    for name, factor in factors.items():
        out[name] = (out[name] * factor).astype(out[name].dtype)
    return out
```

```python
from contextlib import ExitStack

import concourse.bass as bass
from concourse import mybir

P = 128
SEQ, D_MODEL = 512, 1024
TILES = SEQ // P
KT = D_MODEL // P
ATT_HEADS, ATT_HD = 8, 64
IDX_HEADS, IDX_HD = 4, 64
GLA_HEADS, GLA_DK, GLA_DV, GATE_RANK = 4, 64, 128, 16
ATT_W, GLA_W = ATT_HEADS * ATT_HD, GLA_HEADS * GLA_DV
HALF = ATT_HD // 4 // 2
KSEL = SEQ // 4
ROUNDS = KSEL // 8
EPS = 1e-6
NEG = -1e30
TAKEN = -3e38
LEVELS = 7
PI = 3.141592653589793
PI_BELOW = 3.1415925
TWO_PI = (6.28125, 0.0019350051879882812, 3.0199159819e-07)

F32 = mybir.dt.float32
F32R = mybir.dt.float32r
I32 = mybir.dt.int32
U8 = mybir.dt.uint8
ALU = mybir.AluOpType
ACT = mybir.ActivationFunctionType
AX = mybir.AxisListType

CHUNKS = [
    [(1536, 324), (3396, 16)],
    [(0, 512)],
    [(512, 512)],
    [(2372, 512)],
    [(1024, 512)],
    [(1860, 512)],
    [(2884, 512)],
    [(3412, 512)],
]
C_IDX, C_AQ, C_AK, C_GQK, C_AV, C_AGATE, C_GV, C_GGATE = range(8)
NC = len(CHUNKS)
WIDTH = [sum(w for _, w in c) for c in CHUNKS]
WOUT_PIECES = 4
LR0, IW0 = 384, 400
IDENT, CUM, REV, CAUSAL, FREQ, NCONST = 0, 128, 256, 384, 512, 520

GENERAL = [4, 5, 6]
GENERAL_LATE = [4, 5, 6, 0, 1]
OUT_BANKS = [2, 3]
O_BANK = 7


def pT_on_act(u):
    return u % 2 == 0


def units(tiles):
    return [(t, h) for t in tiles for h in range(ATT_HEADS)]


def schedule():
    plan = []
    add = plan.append
    fill = {}

    def at(c, half, t, *steps):
        fill.setdefault((c, half, t), []).extend(steps)

    for t in range(TILES):
        at(C_AQ, 0, t // 2, ("idxT", t))
        at(C_AQ, 1, t, ("gz", t))
        at(C_AK, 0, t, ("rowT", C_AQ, t))
        at(C_GQK, 0, t, ("rowT", C_AK, t))
        at(C_AK, 1, t, ("cum", t))
        at(C_AV, 0, t, ("rowT", C_GQK, t))
        at(C_GGATE, 0, t, ("kv", t))
    for t in range(1, TILES):
        at(C_AQ, 0 if t < 3 else 1, (t + 1) % 4, *[("score", t, h) for h in range(IDX_HEADS)])
    at(C_AK, 0, 1, ("logalpha",))
    groups = [(c, half, t) for c in range(NC) for half in range(2) for t in range(TILES)]
    rounds = [("topk", t, r) for t in range(1, TILES) for r in range(ROUNDS)]
    g = groups.index((C_AQ, 1, 0))
    while rounds:
        at(*groups[g], *rounds[:3])
        rounds = rounds[3:]
        g += 1
    at(C_AV, 1, 0, ("qkdiag",), ("qinter",))
    g = groups.index((C_AV, 1, 0))
    for n in range(LEVELS * GLA_HEADS):
        lev, h = divmod(n, GLA_HEADS)
        if h == 0:
            at(*groups[g], ("level", lev))
        at(*groups[g], ("pairs", lev, h))
        if n % 2 == 1:
            g += 1
    todo = units(range(TILES - 1))
    g = groups.index((C_AGATE, 0, 0))
    for u in todo:
        at(*groups[g], ("unit", *u))
        g += 1
    for n in range(2 * TILES):
        if n < 2:
            add(("prep", n))
    for t in range(TILES):
        for g2 in range(2):
            add(("xT", t, g2))
    add(("angles",))
    for t in range(TILES):
        add(("ssq", t))
    for c, half, t in groups:
        add(("proj", c, half, t))
        n = 2 * c + half
        if t == 0 and 0 < n < 2 * NC - 1:
            add(("prep", n + 1))
        if half == 1:
            add(("evac", c, t))
        plan.extend(fill.get((c, half, t), []))
    post = units([TILES - 1])
    for n in range(4):
        add(("wprep", n))
        add(("unit", *post[2 * n]))
        add(("unit", *post[2 * n + 1]))
        add(("glaout", n))
        add(("glafin", n))
    for t in range(TILES):
        for g2 in range(2):
            add(("mixT", t, g2))
        add(("outp", t))
        add(("fin", t))
    out, made = [], []

    def late(made_now):
        k = made_now
        if 0 <= k - 1 < len(made):
            out.append(("pT", *made[k - 1]))
        if 0 <= k - 2 < len(made):
            pv(made[k - 2])

    def pv(u):
        out.append(("pv", *u))
        if u[1] == ATT_HEADS - 1:
            out.append(("attfin", u[0]))

    for s in plan:
        if s[0] == "unit":
            made.append(s[1:])
            out.append(("qk", *s[1:]))
            late(len(made) - 1)
            if len(made) == len(units(range(TILES))):
                late(len(made))
                late(len(made) + 1)
        else:
            out.append(s)
    return out


def psum_jobs(plan):
    jobs, used, ring = {}, [0] * 8, 0

    def take(key, bank):
        jobs[key] = (bank, used[bank])
        used[bank] += 1

    late = False
    for s in plan:
        if s[0] == "proj" and s[2] == 0:
            take(("proj", s[1], s[3]), s[3])
        elif s[0] in ("xT", "idxT", "score", "gz", "rowT", "cum", "pairs", "kv", "qk", "pT", "mixT"):
            if s[0] == "kv" and s[1] == TILES - 1:
                continue
            banks = GENERAL_LATE if late else GENERAL
            take(s, banks[ring % len(banks)])
            ring += 1
        elif s[0] == "glaout":
            for odd in range(2):
                take((*s, odd), GENERAL_LATE[ring % len(GENERAL_LATE)])
                ring += 1
        elif s[0] == "pv" and s[2] == 0:
            take(("att", s[1]), O_BANK)
        elif s[0] == "outp":
            for n, b in enumerate(OUT_BANKS):
                take(("outp", s[1], n), b)
        if s[0] == "wprep":
            if not late:
                ring = 0
            late = True
    return jobs


def layer_kernel(nc, x, positions, w_in, w_up, b_gate, gla_norm_w, w_out, pre_norm_w, post_norm_w,
                 consts, level_masks, out):
    plan = schedule()
    jobs = psum_jobs(plan)
    UNITS = [s[1:] for s in plan if s[0] == "qk"]
    unit_no = {u: n for n, u in enumerate(UNITS)}
    PAIRS = [s[1:] for s in plan if s[0] == "pairs"]
    x_v = x.rearrange("b (t p) d -> (b t) p d", p=P)
    out_v = out.rearrange("b (t p) d -> (b t) p d", p=P)
    w_in_v = w_in.rearrange("(p k) n -> p k n", k=KT)
    w_out_v = w_out.rearrange("(p k) n -> p k n", k=KT)

    with ExitStack() as ctx:
        place = [(nc.sbuf_base + 63) // 32 * 32]

        def put(name, shape, dt=F32, offset=None):
            size = {F32: 4, F32R: 4, I32: 4, U8: 1}[dt]
            for n in shape[1:]:
                size *= n
            at = place[0] if offset is None else offset
            if offset is None:
                place[0] += (size + 31) // 32 * 32
            return nc.alloc_sbuf_tensor_at(name, shape, dt, offset=at), at

        def sb(name, shape, dt=F32, offset=None):
            return put(name, shape, dt, offset)[0]

        def sem(name):
            return ctx.enter_context(nc.semaphore(name))

        cst = sb("cst", [P, NCONST])
        lvl = sb("lvl", [P, LEVELS, P], U8)
        prew = sb("prew", [P, KT])
        glaw = sb("glaw", [P, GLA_DV])
        bgate = sb("bgate", [P, GLA_HEADS * GLA_DK])
        wup = sb("wup", [GATE_RANK, GLA_HEADS * GLA_DK])
        pos = sb("pos", [P, TILES], I32)
        ang = sb("ang", [P, 4, TILES, HALF])
        cosd = sb("cosd", [P, TILES, 2, HALF])
        sind = sb("sind", [P, TILES, 2, HALF])
        ropet = sb("ropet", [P, 2, ATT_HEADS, 2 * HALF])
        ssq = sb("ssq", [P, 4, TILES])
        iw = sb("iw", [P, TILES, IDX_HEADS])
        best = sb("best", [P, 8])
        nmax = sb("nmax", [P, TILES * ATT_HEADS])
        psums = sb("psums", [P, TILES * ATT_HEADS])
        rinv = sb("rinv", [P, TILES * ATT_HEADS])
        qkd = sb("qkd", [P, 2, TILES * GLA_HEADS])
        dec = sb("dec", [P, 2, TILES])
        gss = sb("gss", [P, 3, TILES * GLA_HEADS])
        oss = sb("oss", [P, 5, TILES])
        pwr = sb("pwr", [P, 1])
        xm = sb("xm", [P, TILES, D_MODEL])
        hT_hi = sb("hT_hi", [P, KT, SEQ], F32R)
        hT_lo = sb("hT_lo", [P, KT, SEQ], F32R)
        w_hi = sb("w_hi", [P, 2, KT // 2, 512], F32R)
        w_lo = sb("w_lo", [P, 2, KT // 2, 512], F32R)
        raw = sb("raw", [P, 2, KT // 2, 512])
        aqT = sb("aqT", [P, 4, SEQ])
        akT = sb("akT", [P, 4, SEQ])
        av = sb("av", [P, TILES, ATT_W])
        row, row_at = put("row", [P, TILES, 512])
        X = sb("X", [P, 2, 2, SEQ], offset=row_at)
        mT_hi = sb("mT_hi", [P, 2, KT, P], F32R, offset=row_at)
        idxrow, idx_at = put("idxrow", [P, TILES, 512])
        idxT = sb("idxT", [P, 4, SEQ])
        gqkT = sb("gqkT", [P, 4, SEQ], offset=idx_at)
        bT = sb("bT", [P, 2, SEQ], offset=idx_at + 8192)
        qi = sb("qi", [P, 2, SEQ], offset=idx_at + 12288)
        yout = sb("yout", [P, 2, D_MODEL], offset=idx_at)
        xre = sb("xre", [P, 2, D_MODEL], offset=idx_at + 8192)
        work, work_at = put("work", [P, 1152])
        postw = sb("postw", [P, D_MODEL], offset=work_at)
        bias = sb("bias", [P, 1280])
        grow, grow_at = put("grow", [P, TILES, 512])
        mT_lo = sb("mT_lo", [P, 2, KT, P], F32R, offset=grow_at)
        gv = sb("gv", [P, TILES, GLA_W])
        lg, lg_at = put("lg", [P, TILES, 256])
        og = sb("og", [P, 512], offset=lg_at)
        attn = sb("attn", [P, 512], offset=lg_at + 2048)
        Pb, p_at = put("Pb", [P, 2, 512])
        lgt = sb("lgt", [P, TILES, 256], offset=p_at)
        pTb, pt_at = put("pTb", [P, 2, 512])
        rel = sb("rel", [P, 2, 512], offset=pt_at)
        E = sb("E", [P, 2, SEQ])
        AT, at_at = put("AT", [P, GLA_HEADS, TILES, P])
        lvl_in = sb("lvl_in", [P, LEVELS, P], I32, offset=at_at)
        S = sb("S", [P, TILES - 1, 2, GLA_DV])
        th = sb("th", [P, 512])
        assert place[0] <= nc.sbuf_usable_end, place[0] - nc.sbuf_usable_end

        bank = [ctx.enter_context(nc.psum_tensor(f"bank{n}", [P, 512], F32)) for n in range(8)]
        full = [sem(f"bank{n}_full") for n in range(8)]
        moved = [sem(f"bank{n}_moved") for n in range(8)]

        d_cst, d_prew, d_small, d_mask, d_pos, d_post = (sem(n) for n in (
            "d_cst", "d_prew", "d_small", "d_mask", "d_pos", "d_post"))
        d_x = [sem(f"d_x{t}") for t in range(TILES)]
        d_raw = [sem(f"d_raw{n}") for n in range(2)]
        d_xre = [sem(f"d_xre{n}") for n in range(2)]
        d_out = [sem(f"d_out{n}") for n in range(2)]
        names = ("a_ssq a_hTh a_whi a_ang a_th a_la a_dec a_E a_p a_gsq a_mTh a_osq a_wo "
                 "v_hTl v_wlo v_ang v_score v_cand v_best v_bias v_lg v_gate v_qk v_qi v_D v_X "
                 "v_gm v_rinv v_am v_y v_wo "
                 "g_init g_rstd g_ropet g_rope g_iw g_kt g_gate g_grs g_ors t_half t_pv").split()
        s = {n: sem(n) for n in names}

        def raw_value(n):
            pieces = [len(CHUNKS[m // 2]) if m < 2 * NC else 1 for m in range(n % 2, n + 1, 2)]
            return 16 * sum(pieces)

        def wait_full(eng, key):
            b, n = jobs[key]
            eng.wait_ge(full[b], n + 1)
            return bank[b]

        def is_free(eng, key):
            b, n = jobs[key]
            if n > 0:
                eng.wait_ge(moved[b], n)
            return bank[b]

        def wait_moved(eng, key):
            b, n = jobs[key]
            eng.wait_ge(moved[b], n + 1)

        def half_done(eng, n):
            c, half = divmod(n, 2)
            if half == 0:
                eng.wait_ge(s["t_half"], c + 1)
            else:
                wait_full(eng, ("proj", c, TILES - 1))

        def pv_done(eng, n):
            t, h = UNITS[n]
            if h == ATT_HEADS - 1:
                wait_full(eng, ("att", t))
            else:
                eng.wait_ge(s["t_pv"], n - t)

        def filled(key):
            return full[jobs[key][0]]

        def emptied(key):
            return moved[jobs[key][0]]

        def ident():
            return cst[:, IDENT:IDENT + P]

        block = ctx.enter_context(nc.Block())

        @block.sync
        def _(sp):
            def load_weights(n):
                if n >= 2:
                    if n - 2 < 2 * NC:
                        sp.wait_ge(s["a_whi"], n - 1)
                        sp.wait_ge(s["v_wlo"], n - 1)
                    else:
                        sp.wait_ge(s["a_wo"], 2 * (n - 1 - 2 * NC))
                        sp.wait_ge(s["v_wo"], 2 * (n - 1 - 2 * NC))
                if n < 2 * NC:
                    c, half = divmod(n, 2)
                    col = 0
                    for first, width in CHUNKS[c]:
                        sp.dma_start(raw[:, n % 2, :, col:col + width],
                                     w_in_v[:, half * KT // 2:(half + 1) * KT // 2, first:first + width]
                                     ).then_inc(d_raw[n % 2], 16)
                        col += width
                else:
                    j = n - 2 * NC
                    sp.dma_start(raw[:, n % 2, :, :].rearrange("p k n -> p (k n)"),
                                 w_out_v[:, 2 * j:2 * j + 2, :].rearrange("p k n -> p (k n)")
                                 ).then_inc(d_raw[n % 2], 16)

            sp.dma_start(xm[:, 0, :], x_v[0]).then_inc(d_x[0], 16)
            sp.dma_start(cst[:, :], consts).then_inc(d_cst, 16)
            load_weights(0)
            sp.dma_start(xm[:, 1, :], x_v[1]).then_inc(d_x[1], 16)
            load_weights(1)
            for t in range(2, TILES):
                sp.dma_start(xm[:, t, :], x_v[t]).then_inc(d_x[t], 16)
            sp.dma_start(lvl_in[:, :, :], level_masks).then_inc(d_mask, 16)
            for n in range(2, 2 * NC + WOUT_PIECES):
                load_weights(n)
            sp.wait_ge(s["v_bias"], TILES - 1)
            sp.dma_start(postw[:, :], post_norm_w.partition_broadcast(P)).then_inc(d_post, 16)
            wait_moved(sp, ("glaout", TILES - 1, 1))
            for t in range(TILES):
                if t >= 2:
                    sp.wait_ge(s["v_y"], t - 1)
                sp.dma_start(xre[:, t % 2, :], x_v[t]).then_inc(d_xre[t % 2], 16)
            for t in range(TILES):
                sp.wait_ge(s["v_y"], t + 1)
                sp.dma_start(out_v[t], yout[:, t % 2, :]).then_inc(d_out[t % 2], 16)
            for n in range(2):
                sp.wait_ge(d_out[n], 16 * TILES // 2)

        @block.tensor
        def _(pe):
            def xT(t, g):
                if g == 0:
                    pe.wait_ge(d_x[t], 16)
                    if t == 0:
                        pe.wait_ge(d_cst, 16)
                b = is_free(pe, ("xT", t, g))
                for j in range(4):
                    k = 4 * g + j
                    last = nc.tensor.transpose(b[:, P * j:P * (j + 1)], xm[:, t, k::KT], ident())
                last.then_inc(filled(("xT", t, g)), 1)

            def proj(c, half, t):
                n, w = 2 * c + half, WIDTH[c]
                b = bank[t]
                if t == 0:
                    pe.wait_ge(s["a_whi"], n + 1)
                    pe.wait_ge(s["v_wlo"], n + 1)
                if n == 0:
                    pe.wait_ge(s["v_hTl"], 2 * (t + 1))
                if half == 0:
                    is_free(pe, ("proj", c, t))
                for j in range(KT // 2):
                    k = half * (KT // 2) + j
                    h_hi, h_lo = (a[:, k, P * t:P * (t + 1)] for a in (hT_hi, hT_lo))
                    v_hi, v_lo = (a[:, n % 2, j, 0:w] for a in (w_hi, w_lo))
                    nc.tensor.matmul(b[:, 0:w], h_hi, v_hi, start=(k == 0), stop=False)
                    nc.tensor.matmul(b[:, 0:w], h_hi, v_lo, start=False, stop=False)
                    last = nc.tensor.matmul(b[:, 0:w], h_lo, v_hi, start=False, stop=(k == KT - 1))
                if half == 1:
                    last.then_inc(full[t], 1)
                if half == 0 and t == TILES - 1:
                    last.then_inc(s["t_half"], 1)

            def idxT_(t):
                pe.wait_ge(s["g_rope"], t + 1)
                b = is_free(pe, ("idxT", t))
                for j in range(4):
                    last = nc.tensor.transpose(b[:, P * j:P * (j + 1)], idxrow[:, t, P * j:P * (j + 1)], ident())
                last.then_inc(filled(("idxT", t)), 1)

            def score(t, h):
                n = (t + 1) * P
                if h == 0:
                    wait_moved(pe, ("idxT", t))
                b = is_free(pe, ("score", t, h))
                lo = 64 * (h % 2)
                nc.tensor.matmul(b[:, 0:n], idxT[lo:lo + 64, h // 2, P * t:P * (t + 1)], idxT[lo:lo + 64, 2, 0:n],
                                 start=True, stop=True).then_inc(filled(("score", t, h)), 1)

            def gz(t):
                wait_moved(pe, ("idxT", t))
                if t == 0:
                    pe.wait_ge(d_small, 48)
                b = is_free(pe, ("gz", t))
                nc.tensor.matmul(b[:, 0:256], idxT[0:GATE_RANK, 3, P * t:P * (t + 1)], wup[:, :],
                                 start=True, stop=True).then_inc(filled(("gz", t)), 1)

            def rowT(c, t):
                src = row if c != C_GQK else grow
                if c == C_GQK:
                    wait_moved(pe, ("proj", c, t))
                else:
                    pe.wait_ge(s["g_rope"], TILES * c + t + 1)
                b = is_free(pe, ("rowT", c, t))
                for j in range(4):
                    last = nc.tensor.transpose(b[:, P * j:P * (j + 1)], src[:, t, P * j:P * (j + 1)], ident())
                last.then_inc(filled(("rowT", c, t)), 1)

            def cum(t):
                pe.wait_ge(s["v_lg"], 1)
                b = is_free(pe, ("cum", t))
                for g in range(2):
                    nc.tensor.matmul(b[:, P * g:P * (g + 1)], lg[:, t, P * g:P * (g + 1)], cst[:, CUM:CUM + P],
                                     start=True, stop=True)
                nc.tensor.matmul(b[:, 256:512], cst[:, REV:REV + P], lg[:, t, :],
                                 start=True, stop=True).then_inc(filled(("cum", t)), 1)

            def pairs(lev, h):
                pe.wait_ge(s["v_X"], 2 * (lev + 1))
                b = is_free(pe, ("pairs", lev, h))
                lo = 64 * (h % 2)
                for t in range(TILES):
                    xt = X[lo:lo + 64, lev % 2, h // 2, P * t:P * (t + 1)]
                    last = nc.tensor.matmul(b[:, P * t:P * (t + 1)], xt, xt, start=True, stop=True)
                last.then_inc(filled(("pairs", lev, h)), 1)

            def kv(t):
                if t == TILES - 1:
                    return
                pe.wait_ge(s["g_kt"], t + 1)
                wait_moved(pe, ("proj", C_GV, t))
                b = is_free(pe, ("kv", t))
                for h in range(GLA_HEADS):
                    lo = 64 * (h % 2)
                    last = nc.tensor.matmul(b[lo:lo + 64, P * (h // 2):P * (h // 2 + 1)],
                                            grow[:, t, 256 + 64 * h:256 + 64 * (h + 1)],
                                            gv[:, t, P * h:P * (h + 1)], start=True, stop=True)
                last.then_inc(filled(("kv", t)), 1)

            def glaout(t):
                for h in range(GLA_HEADS):
                    wait_moved(pe, ("pairs", LEVELS - 1, h))
                pe.wait_ge(s["v_qi"], 1)
                if t > 0:
                    wait_moved(pe, ("kv", t - 1))
                for odd in range(2):
                    key = ("glaout", t, odd)
                    b = is_free(pe, key)
                    for h in range(odd, GLA_HEADS, 2):
                        lo, o = 64 * odd, b[:, P * (h // 2):P * (h // 2 + 1)]
                        last = nc.tensor.matmul(o, AT[:, h, t, :], gv[:, t, P * h:P * (h + 1)],
                                                start=True, stop=(t == 0))
                        if t > 0:
                            last = nc.tensor.matmul(o, qi[lo:lo + 64, h // 2, P * t:P * (t + 1)],
                                                    S[lo:lo + 64, t - 1, h // 2, :], start=False, stop=True)
                    last.then_inc(filled(key), 1)

            def qk_(t, h):
                n, lo = (t + 1) * P, 64 * (h % 2)
                if h == 0:
                    wait_moved(pe, ("rowT", C_AK, TILES - 1))
                b = is_free(pe, ("qk", t, h))
                nc.tensor.matmul(b[:, 0:n], aqT[lo:lo + 64, h // 2, P * t:P * (t + 1)], akT[lo:lo + 64, h // 2, 0:n],
                                 start=True, stop=True).then_inc(filled(("qk", t, h)), 1)

            def pT(t, h):
                u = unit_no[(t, h)]
                pe.wait_ge(s["a_p"], u + 1)
                b = is_free(pe, ("pT", t, h))
                for j in range(t + 1):
                    last = nc.tensor.transpose(b[:, P * j:P * (j + 1)], Pb[:, u % 2, P * j:P * (j + 1)], ident())
                last.then_inc(filled(("pT", t, h)), 1)

            def pv(t, h):
                u = unit_no[(t, h)]
                wait_moved(pe, ("pT", t, h))
                if h == 0:
                    wait_moved(pe, ("proj", C_AV, t))
                    is_free(pe, ("att", t))
                b = bank[O_BANK]
                for j in range(t + 1):
                    last = nc.tensor.matmul(b[:, 64 * h:64 * (h + 1)], pTb[:, u % 2, P * j:P * (j + 1)],
                                            av[:, j, 64 * h:64 * (h + 1)], start=(j == 0), stop=(j == t))
                if h == ATT_HEADS - 1:
                    last.then_inc(full[O_BANK], 1)
                else:
                    last.then_inc(s["t_pv"], 1)

            def mixT(t, g):
                pe.wait_ge(s["v_am"], t + 1)
                pe.wait_ge(s["v_gm"], GLA_HEADS * (t + 1))
                b = is_free(pe, ("mixT", t, g))
                for j in range(4):
                    last = nc.tensor.transpose(b[:, P * j:P * (j + 1)], xm[:, t, 4 * g + j::KT], ident())
                last.then_inc(filled(("mixT", t, g)), 1)

            def outp(t):
                if t == 0:
                    pe.wait_ge(s["a_wo"], 2 * WOUT_PIECES)
                    pe.wait_ge(s["v_wo"], 2 * WOUT_PIECES)
                wait_moved(pe, ("mixT", t, 0))
                wait_moved(pe, ("mixT", t, 1))
                for n in range(2):
                    b = is_free(pe, ("outp", t, n))
                    for k in range(KT):
                        m_hi, m_lo = (a[:, t % 2, k, :] for a in (mT_hi, mT_lo))
                        if n == 0:
                            v_hi, v_lo = hT_hi[:, k, :], hT_lo[:, k, :]
                        else:
                            v_hi, v_lo = (a[:, k // 4, k % 4, :] for a in (w_hi, w_lo))
                        nc.tensor.matmul(b[:, :], m_hi, v_hi, start=(k == 0), stop=False)
                        nc.tensor.matmul(b[:, :], m_hi, v_lo, start=False, stop=False)
                        last = nc.tensor.matmul(b[:, :], m_lo, v_hi, start=False, stop=(k == KT - 1))
                    last.then_inc(full[OUT_BANKS[n]], 1)

            parts = {"xT": xT, "proj": proj, "idxT": idxT_, "score": score, "gz": gz, "rowT": rowT, "cum": cum,
                     "pairs": pairs, "kv": kv, "glaout": glaout, "qk": qk_, "pT": pT, "pv": pv, "mixT": mixT,
                     "outp": outp}
            for step in plan:
                if step[0] in parts:
                    parts[step[0]](*step[1:])

        @block.scalar
        def _(act):
            act.dma_start(prew[:, :], pre_norm_w.rearrange("(p k) -> p k", k=KT)).then_inc(d_prew, 16)
            act.dma_start(pos[:, :], positions).then_inc(d_pos, 16)
            act.dma_start(wup[:, :], w_up).then_inc(d_small, 16)
            act.dma_start(bgate[:, :], b_gate.partition_broadcast(P)).then_inc(d_small, 16)
            act.dma_start(glaw[:, :], gla_norm_w.partition_broadcast(P)).then_inc(d_small, 16)
            def angles():
                act.wait_ge(s["v_ang"], 9)
                nc.scalar.activation(sind[:, :, 1, :], ang[:, 2, :, :], ACT.Sin).then_inc(s["a_ang"], 1)
                nc.scalar.activation(cosd[:, :, 0, :], ang[:, 3, :, :], ACT.Sin).then_inc(s["a_ang"], 1)
                act.wait_ge(s["a_ang"], 2)
                nc.scalar.activation(sind[:, :, 0, :], sind[:, :, 1, :], ACT.Copy, scale=-1.0).then_inc(s["a_ang"], 1)
                nc.scalar.activation(cosd[:, :, 1, :], cosd[:, :, 0, :], ACT.Copy).then_inc(s["a_ang"], 1)

            def prep(n):
                w = WIDTH[n // 2]
                act.wait_ge(d_raw[n % 2], raw_value(n))
                if n >= 2:
                    half_done(act, n - 2)
                nc.scalar.activation(w_hi[:, n % 2, :, 0:w], raw[:, n % 2, :, 0:w], ACT.Copy).then_inc(s["a_whi"], 1)

            def xT(t, g):
                j = 2 * t + g
                wait_moved(act, ("xT", t, g))
                nc.scalar.activation(hT_hi[:, 4 * g:4 * g + 4, P * t:P * (t + 1)],
                                     row[:, j % 4, :].rearrange("p (k n) -> p k n", k=4),
                                     ACT.Copy).then_inc(s["a_hTh"], 1)

            def ssq_(t):
                act.wait_ge(d_x[t], 16)
                if t > 0:
                    act.wait_ge(s["a_ssq"], t)
                nc.scalar.activation(E[:, :, :].rearrange("p a b -> p (a b)"), xm[:, t, :], ACT.Square,
                                     accum_out=ssq[:, 0, t:t + 1]).then_inc(s["a_ssq"], 1)

            def evac(c, t):
                key = ("proj", c, t)
                b = wait_full(act, key)
                rstd, hrstd = ssq[:, 2, t:t + 1], ssq[:, 3, t:t + 1]
                act.wait_ge(s["g_rstd"], 3)
                if c == C_IDX:
                    nc.scalar.activation(idxrow[:, t, 0:320], b[:, 0:320], ACT.Copy, scale=rstd)
                    nc.scalar.activation(idxrow[:, t, IW0:IW0 + 4], b[:, 320:324], ACT.Copy, scale=rstd)
                    nc.scalar.activation(idxrow[:, t, LR0:LR0 + GATE_RANK], b[:, 324:340], ACT.Copy, scale=rstd)\
                        .then_inc(emptied(key), 1)
                elif c in (C_AGATE, C_GGATE):
                    o = 0 if c == C_AGATE else ATT_W
                    before = t + (TILES if c == C_GGATE else 0)
                    if before > 0:
                        act.wait_ge(s["v_gate"], before)
                    nc.scalar.activation(th[:, :], b[:, :], ACT.Tanh, scale=hrstd)
                    nc.scalar.activation(xm[:, t, o:o + 512], b[:, :], ACT.Copy, scale=hrstd).then_inc(emptied(key), 1)
                else:
                    dst = {C_AQ: row, C_AK: row, C_GQK: grow, C_AV: av, C_GV: gv}[c]
                    nc.scalar.activation(dst[:, t, :], b[:, :], ACT.Copy, scale=rstd).then_inc(emptied(key), 1)

            def idxT_(t):
                key = ("idxT", t)
                b = wait_full(act, key)
                nc.scalar.activation(idxT[:, :, P * t:P * (t + 1)], b[:, :].rearrange("p (k n) -> p k n", k=4),
                                     ACT.Copy).then_inc(emptied(key), 1)

            def score(t, h):
                key, n, i = ("score", t, h), (t + 1) * P, IDX_HEADS * (t - 1) + h
                b = wait_full(act, key)
                if i >= 2:
                    act.wait_ge(s["v_score"], (i - 2) // IDX_HEADS * 5 + (i - 2) % IDX_HEADS + 1)
                nc.scalar.activation(rel[:, i % 2, 0:n], b[:, 0:n], ACT.Relu).then_inc(emptied(key), 1)

            def logalpha():
                for t in range(TILES):
                    wait_moved(act, ("gz", t))
                nc.scalar.activation(lgt[:, :, :], lg[:, :, :], ACT.Abs).then_inc(s["a_la"], 1)
                act.wait_ge(s["a_la"], 1)
                nc.scalar.activation(lgt[:, :, :], lgt[:, :, :], ACT.Exp, scale=-1.0).then_inc(s["a_la"], 1)
                act.wait_ge(s["a_la"], 2)
                nc.scalar.activation(lgt[:, :, :], lgt[:, :, :], ACT.Ln, bias=1.0).then_inc(s["a_la"], 1)

            def cum(t):
                key = ("cum", t)
                b = wait_full(act, key)
                nc.scalar.activation(bT[:, :, P * t:P * (t + 1)], b[:, 0:256].rearrange("p (g n) -> p g n", g=2),
                                     ACT.Copy)
                nc.scalar.activation(lg[:, t, :], b[:, 256:512], ACT.Exp, scale=1 / 16).then_inc(emptied(key), 1)

            def rowT(c, t):
                key = ("rowT", c, t)
                b = wait_full(act, key)[:, :].rearrange("p (k n) -> p k n", k=4)
                if c == C_GQK:
                    nc.scalar.activation(gqkT[:, 0:2, P * t:P * (t + 1)], b[:, 0:2, :], ACT.Copy, scale=GLA_DK ** -0.5)
                    nc.scalar.activation(gqkT[:, 2:4, P * t:P * (t + 1)], b[:, 2:4, :], ACT.Copy)\
                        .then_inc(emptied(key), 1)
                else:
                    dst = aqT if c == C_AQ else akT
                    nc.scalar.activation(dst[:, :, P * t:P * (t + 1)], b, ACT.Copy).then_inc(emptied(key), 1)

            def exp_level(lev):
                half = P // 2 >> lev
                e = E[:, :, :].rearrange("p g (n i) -> p (g n) i", i=2 * half)
                act.wait_ge(s["v_D"], lev + 1)
                nc.scalar.activation(e[:, :, 0:half], e[:, :, 0:half], ACT.Exp, scale=-1 / 16).then_inc(s["a_E"], 1)
                nc.scalar.activation(e[:, :, half:], e[:, :, half:], ACT.Exp, scale=1 / 16).then_inc(s["a_E"], 1)

            def qinter():
                act.wait_ge(s["v_qk"], 3)
                nc.scalar.activation(E[:, :, :], bT[:, :, :], ACT.Exp, scale=1 / 16).then_inc(s["a_dec"], 1)
                act.wait_ge(s["a_dec"], 1)
                nc.scalar.activation(dec[:, :, :], E[:, :, P - 1::P], ACT.Copy).then_inc(s["a_dec"], 1)
                exp_level(0)

            def level(lev):
                if lev + 1 < LEVELS:
                    exp_level(lev + 1)

            def qk_(t, h):
                u, n = unit_no[(t, h)], (t + 1) * P
                wait_moved(act, ("qk", t, h))
                nc.scalar.activation(Pb[:, u % 2, 0:n], Pb[:, u % 2, 0:n], ACT.Exp, bias=nmax[:, u:u + 1], scale=-1.0,
                                     accum_out=psums[:, u:u + 1]).then_inc(s["a_p"], 1)

            def pT(t, h):
                u, n, key = unit_no[(t, h)], (t + 1) * P, ("pT", t, h)
                if not pT_on_act(u):
                    return
                b = wait_full(act, key)
                if u >= 2:
                    pv_done(act, u - 2)
                nc.scalar.activation(pTb[:, u % 2, 0:n], b[:, 0:n], ACT.Copy).then_inc(emptied(key), 1)

            def glaout(t):
                wait_moved(act, ("glaout", t, 0))
                wait_moved(act, ("glaout", t, 1))
                for h in range(GLA_HEADS):
                    if GLA_HEADS * t + h > 0:
                        act.wait_ge(s["a_gsq"], GLA_HEADS * t + h)
                    nc.scalar.activation(E[:, 0, 0:P], og[:, P * h:P * (h + 1)], ACT.Square,
                                         accum_out=gss[:, 0, GLA_HEADS * t + h:GLA_HEADS * t + h + 1])\
                        .then_inc(s["a_gsq"], 1)

            def wprep(j):
                act.wait_ge(d_raw[j % 2], raw_value(2 * NC + j))
                if j == 0:
                    wait_full(act, ("proj", NC - 1, TILES - 1))
                src = raw[:, j % 2, :, :].rearrange("p (k m) n -> p k (m n)", k=2)
                k = 2 * j
                nc.scalar.activation(hT_hi[:, k:k + 2, :], src[:, :, 0:512], ACT.Copy).then_inc(s["a_wo"], 1)
                nc.scalar.activation(w_hi[:, k // 4, k % 4:k % 4 + 2, :], src[:, :, 512:1024], ACT.Copy)\
                    .then_inc(s["a_wo"], 1)

            def mixT(t, g):
                b = wait_full(act, ("mixT", t, g))
                if t >= 2:
                    wait_full(act, ("outp", t - 2, 1))
                nc.scalar.activation(mT_hi[:, t % 2, 4 * g:4 * g + 4, :], b[:, :].rearrange("p (k n) -> p k n", k=4),
                                     ACT.Copy).then_inc(s["a_mTh"], 1)

            def outp(t):
                for n in range(2):
                    b = wait_full(act, ("outp", t, n))
                    if 2 * t + n > 0:
                        act.wait_ge(s["a_osq"], 2 * t + n)
                    nc.scalar.activation(E[:, n, :], b[:, :], ACT.Square, accum_out=oss[:, n, t:t + 1])\
                        .then_inc(s["a_osq"], 1)

            parts = {"prep": prep, "xT": xT, "ssq": ssq_, "angles": angles, "evac": evac, "idxT": idxT_, "score": score,
                     "logalpha": logalpha, "cum": cum, "rowT": rowT, "qinter": qinter, "level": level, "qk": qk_,
                     "pT": pT, "glaout": glaout, "wprep": wprep, "mixT": mixT, "outp": outp}
            for step in plan:
                if step[0] in parts:
                    parts[step[0]](*step[1:])

        @block.vector
        def _(dve):
            V = nc.vector

            def angles():
                a, turns, r, c = (ang[:, n, :, :] for n in range(4))
                magic = 1.5 * 2.0 ** 23
                steps = [
                    lambda: V.tensor_tensor(a, pos[:, :].unsqueeze(2).broadcast_to([P, TILES, HALF]),
                                            cst[:, FREQ:FREQ + HALF].unsqueeze(1).broadcast_to([P, TILES, HALF]),
                                            ALU.mult),
                    lambda: V.tensor_scalar(turns, a, 1 / (2 * PI), magic, ALU.mult, ALU.add),
                    lambda: V.tensor_scalar(turns, turns, -magic, None, ALU.add),
                    lambda: V.scalar_tensor_tensor(r, turns, -TWO_PI[0], a, ALU.mult, ALU.add),
                    lambda: V.scalar_tensor_tensor(r, turns, -TWO_PI[1], r, ALU.mult, ALU.add),
                    lambda: V.scalar_tensor_tensor(r, turns, -TWO_PI[2], r, ALU.mult, ALU.add),
                    lambda: V.tensor_scalar(r, r, PI_BELOW, -PI_BELOW, ALU.min, ALU.max),
                    lambda: V.scalar_tensor_tensor(c, r, -1.0, r, ALU.mult, ALU.min),
                    lambda: V.tensor_scalar(c, c, PI / 2, None, ALU.add),
                ]
                dve.wait_ge(d_pos, 16)
                dve.wait_ge(d_cst, 16)
                for n, step in enumerate(steps):
                    if n > 0:
                        dve.wait_ge(s["v_ang"], n)
                    step().then_inc(s["v_ang"], 1)

            def low_h(j):
                t, g = divmod(j, 2)
                dve.wait_ge(s["a_hTh"], j + 1)
                at = (slice(None), slice(4 * g, 4 * g + 4), slice(P * t, P * (t + 1)))
                V.tensor_tensor(hT_lo[at], row[:, j % 4, :].rearrange("p (k n) -> p k n", k=4),
                                hT_hi[at].bitcast(F32), ALU.subtract).then_inc(s["v_hTl"], 1)

            def xT(t, g):
                key, j = ("xT", t, g), 2 * t + g
                b = wait_full(dve, key)
                if j == 0:
                    dve.wait_ge(d_prew, 16)
                V.tensor_tensor(row[:, j % 4, :].rearrange("p (k n) -> p k n", k=4),
                                b[:, :].rearrange("p (k n) -> p k n", k=4),
                                prew[:, 4 * g:4 * g + 4].unsqueeze(2).broadcast_to([P, 4, P]),
                                ALU.mult).then_inc(emptied(key), 1)
                if j > 0:
                    low_h(j - 1)
                if j == 2 * TILES - 1:
                    low_h(j)

            def prep(n):
                w = WIDTH[n // 2]
                dve.wait_ge(s["a_whi"], n + 1)
                V.tensor_tensor(w_lo[:, n % 2, :, 0:w], raw[:, n % 2, :, 0:w], w_hi[:, n % 2, :, 0:w].bitcast(F32),
                                ALU.subtract).then_inc(s["v_wlo"], 1)

            def evac(c, t):
                if c not in (C_AGATE, C_GGATE):
                    return
                o = 0 if c == C_AGATE else ATT_W
                wait_moved(dve, ("proj", c, t))
                g = xm[:, t, o:o + 512]
                V.scalar_tensor_tensor(g, th[:, :], 1.0, g, ALU.add, ALU.mult).then_inc(s["v_gate"], 1)

            def cand(t):
                at = sum((u + 1) * P for u in range(1, t))
                return work[:, at:at + (t + 1) * P]

            def bias_of(t):
                if t == 0:
                    return cst[:, CAUSAL:CAUSAL + P]
                at = sum((u + 1) * P for u in range(1, t))
                return bias[:, at:at + (t + 1) * P]

            def score(t, h):
                n, i = (t + 1) * P, IDX_HEADS * (t - 1) + h
                wait_moved(dve, ("score", t, h))
                dst, wt = cand(t), iw[:, t, h:h + 1]
                if h == 0:
                    V.tensor_scalar(dst, rel[:, i % 2, 0:n], wt, None, ALU.mult).then_inc(s["v_score"], 1)
                    return
                dve.wait_ge(s["v_score"], 5 * (t - 1) + h)
                V.scalar_tensor_tensor(dst, rel[:, i % 2, 0:n], wt, dst, ALU.mult, ALU.add).then_inc(s["v_score"], 1)
                if h == IDX_HEADS - 1:
                    dve.wait_ge(s["v_score"], 5 * (t - 1) + h + 1)
                    dst = dst[:, t * P:(t + 1) * P]
                    V.tensor_tensor(dst, dst, cst[:, CAUSAL:CAUSAL + P], ALU.add).then_inc(s["v_score"], 1)

            def topk(t, r):
                m = ROUNDS * (t - 1) + r
                if r == 0:
                    dve.wait_ge(s["v_score"], 5 * t)
                if m > 0:
                    dve.wait_ge(s["v_cand"], m)
                V.max(best[:, :], cand(t)).then_inc(s["v_best"], 1)
                dve.wait_ge(s["v_best"], m + 1)
                V.match_replace(cand(t), best[:, :], cand(t), TAKEN).then_inc(s["v_cand"], 1)
                if r == ROUNDS - 1:
                    dve.wait_ge(s["v_cand"], m + 1)
                    V.tensor_scalar(bias_of(t), cand(t), TAKEN, NEG, ALU.is_gt, ALU.mult).then_inc(s["v_bias"], 1)

            def gz(t):
                key = ("gz", t)
                b = wait_full(dve, key)
                if t == 0:
                    dve.wait_ge(d_small, 48)
                V.tensor_tensor(lg[:, t, :], b[:, 0:256], bgate[:, :], ALU.add).then_inc(emptied(key), 1)

            def logalpha():
                dve.wait_ge(s["a_la"], 3)
                V.scalar_tensor_tensor(lg[:, :, :], lg[:, :, :], 0.0, lgt[:, :, :], ALU.min, ALU.subtract)\
                    .then_inc(s["v_lg"], 1)

            def qkdiag():
                for t in range(TILES):
                    wait_moved(dve, ("proj", C_GQK, t))
                prod = E[:, :, :].rearrange("p g (t n) -> p (g t) n", n=256)
                V.tensor_tensor(prod, grow[:, :, 0:256], grow[:, :, 256:512], ALU.mult).then_inc(s["v_qk"], 1)
                dve.wait_ge(s["v_qk"], 1)
                V.tensor_reduce(qkd[:, 0, :], E[:, :, :].rearrange("p g (n d) -> p (g n) d", d=GLA_DK), AX.X,
                                ALU.add).then_inc(s["v_qk"], 1)
                dve.wait_ge(s["v_qk"], 2)
                V.tensor_scalar(qkd[:, 1, :], qkd[:, 0, :], GLA_DK ** -0.5, None, ALU.mult).then_inc(s["v_qk"], 1)

            def blocks(a, half):
                return a.rearrange("p g (n i) -> p (g n) i", i=2 * half)

            def diff(lev):
                half = P // 2 >> lev
                b, e = blocks(bT[:, :, :], half), blocks(E[:, :, :], half)
                n = 2 * SEQ // (2 * half)
                if lev == 0:
                    dve.wait_ge(s["v_qi"], 1)
                else:
                    dve.wait_ge(s["v_X"], 2 * lev)
                V.tensor_tensor(e, b, b[:, :, half - 1:half].broadcast_to([P, n, 2 * half]), ALU.subtract)\
                    .then_inc(s["v_D"], 1)

            def qinter():
                wait_moved(dve, ("rowT", C_GQK, TILES - 1))
                dve.wait_ge(s["a_dec"], 2)
                V.tensor_tensor(qi[:, :, :], gqkT[:, 0:2, :], E[:, :, :], ALU.mult).then_inc(s["v_qi"], 1)
                diff(0)

            def level(lev):
                half = P // 2 >> lev
                e, x = blocks(E[:, :, :], half), blocks(X[:, lev % 2, :, :], half)
                q, k = blocks(gqkT[:, 0:2, :], half), blocks(gqkT[:, 2:4, :], half)
                dve.wait_ge(s["a_E"], 2 * (lev + 1))
                V.tensor_tensor(x[:, :, 0:half], k[:, :, 0:half], e[:, :, 0:half], ALU.mult).then_inc(s["v_X"], 1)
                V.tensor_tensor(x[:, :, half:], q[:, :, half:], e[:, :, half:], ALU.mult).then_inc(s["v_X"], 1)
                if lev + 1 < LEVELS:
                    diff(lev + 1)

            def pairs(lev, h):
                key = ("pairs", lev, h)
                b = wait_full(dve, key)
                if lev == 0 and h == 0:
                    dve.wait_ge(s["g_init"], 4)
                V.copy_predicated(AT[:, h, :, :], lvl[:, lev, :].unsqueeze(1).broadcast_to([P, TILES, P]),
                                  b[:, :].rearrange("p (t n) -> p t n", t=TILES)).then_inc(emptied(key), 1)

            def kv(t):
                if t == TILES - 1:
                    return
                key = ("kv", t)
                b = wait_full(dve, key)
                if t == 0:
                    V.tensor_copy(S[:, 0, :, :], b[:, 0:256].rearrange("p (g n) -> p g n", g=2))\
                        .then_inc(emptied(key), 1)
                    return
                wait_moved(dve, ("kv", t - 1))
                dve.wait_ge(s["a_dec"], 2)
                for g in range(2):
                    last = V.scalar_tensor_tensor(S[:, t, g, :], S[:, t - 1, g, :], dec[:, g, t:t + 1],
                                                  b[:, P * g:P * (g + 1)], ALU.mult, ALU.add)
                last.then_inc(emptied(key), 1)

            def glaout(t):
                dve.wait_ge(s["g_kt"], TILES - 1)
                for odd in range(2):
                    key = ("glaout", t, odd)
                    b = wait_full(dve, key)
                    for h in range(odd, GLA_HEADS, 2):
                        n = GLA_HEADS * t + h
                        last = V.scalar_tensor_tensor(og[:, P * h:P * (h + 1)], gv[:, t, P * h:P * (h + 1)],
                                                      qkd[:, 1, n:n + 1], b[:, P * (h // 2):P * (h // 2 + 1)],
                                                      ALU.mult, ALU.add)
                    last.then_inc(emptied(key), 1)

            def glafin(t):
                dve.wait_ge(s["g_grs"], 2 * (t + 1))
                dve.wait_ge(s["g_gate"], t + 1)
                for h in range(GLA_HEADS):
                    n = GLA_HEADS * t + h
                    g = xm[:, t, ATT_W + P * h:ATT_W + P * (h + 1)]
                    V.scalar_tensor_tensor(g, og[:, P * h:P * (h + 1)], gss[:, 2, n:n + 1], g, ALU.mult, ALU.mult)\
                        .then_inc(s["v_gm"], 1)

            def qk_(t, h):
                u, n, key = unit_no[(t, h)], (t + 1) * P, ("qk", t, h)
                b = wait_full(dve, key)
                if u >= 2:
                    wait_full(dve, ("pT", *UNITS[u - 2]))
                if h == 0 and t > 0:
                    dve.wait_ge(s["v_bias"], t)
                V.tensor_tensor_reduce(Pb[:, u % 2, 0:n], b[:, 0:n], bias_of(t), -ATT_HD ** -0.5, 3e38,
                                       ALU.add, ALU.min, nmax[:, u:u + 1]).then_inc(emptied(key), 1)

            def pT(t, h):
                u, n, key = unit_no[(t, h)], (t + 1) * P, ("pT", t, h)
                if pT_on_act(u):
                    return
                b = wait_full(dve, key)
                if u >= 2:
                    pv_done(dve, u - 2)
                V.tensor_copy(pTb[:, u % 2, 0:n], b[:, 0:n]).then_inc(emptied(key), 1)

            def attfin(t):
                key = ("att", t)
                dve.wait_ge(s["a_p"], ATT_HEADS * (t + 1))
                V.reciprocal(rinv[:, ATT_HEADS * t:ATT_HEADS * (t + 1)], psums[:, ATT_HEADS * t:ATT_HEADS * (t + 1)])\
                    .then_inc(s["v_rinv"], 1)
                b = wait_full(dve, key)
                dve.wait_ge(s["v_rinv"], t + 1)
                dve.wait_ge(s["g_kt"], TILES - 1)
                by_head = "p (h n) -> p h n"
                V.tensor_tensor(attn[:, :].rearrange(by_head, h=ATT_HEADS), b[:, :].rearrange(by_head, h=ATT_HEADS),
                                rinv[:, ATT_HEADS * t:ATT_HEADS * (t + 1)].unsqueeze(2)
                                .broadcast_to([P, ATT_HEADS, ATT_HD]), ALU.mult).then_inc(emptied(key), 1)
                wait_moved(dve, key)
                dve.wait_ge(s["v_gate"], t + 1)
                V.tensor_tensor(xm[:, t, 0:ATT_W], attn[:, :], xm[:, t, 0:ATT_W], ALU.mult).then_inc(s["v_am"], 1)

            def wprep(j):
                src = raw[:, j % 2, :, :].rearrange("p (k m) n -> p k (m n)", k=2)
                k = 2 * j
                dve.wait_ge(s["a_wo"], 2 * j + 1)
                V.tensor_tensor(hT_lo[:, k:k + 2, :], src[:, :, 0:512], hT_hi[:, k:k + 2, :].bitcast(F32),
                                ALU.subtract).then_inc(s["v_wo"], 1)
                dve.wait_ge(s["a_wo"], 2 * j + 2)
                V.tensor_tensor(w_lo[:, k // 4, k % 4:k % 4 + 2, :], src[:, :, 512:1024],
                                w_hi[:, k // 4, k % 4:k % 4 + 2, :].bitcast(F32), ALU.subtract)\
                    .then_inc(s["v_wo"], 1)

            def mixT(t, g):
                key = ("mixT", t, g)
                dve.wait_ge(s["a_mTh"], 2 * t + g + 1)
                b = bank[jobs[key][0]]
                V.tensor_tensor(mT_lo[:, t % 2, 4 * g:4 * g + 4, :], b[:, :].rearrange("p (k n) -> p k n", k=4),
                                mT_hi[:, t % 2, 4 * g:4 * g + 4, :].bitcast(F32), ALU.subtract)\
                    .then_inc(emptied(key), 1)

            def fin(t):
                dve.wait_ge(s["g_ors"], 3 * (t + 1))
                if t == 0:
                    dve.wait_ge(d_post, 16)
                if t >= 2:
                    dve.wait_ge(d_out[t % 2], 16 * (t // 2))
                for n in range(2):
                    y = yout[:, t % 2, 512 * n:512 * (n + 1)]
                    V.scalar_tensor_tensor(y, bank[OUT_BANKS[n]][:, :], oss[:, 4, t:t + 1],
                                           postw[:, 512 * n:512 * (n + 1)], ALU.mult, ALU.mult)\
                        .then_inc(emptied(("outp", t, n)), 1)
                for n in range(2):
                    wait_moved(dve, ("outp", t, n))
                dve.wait_ge(d_xre[t % 2], 16 * (t // 2 + 1))
                V.tensor_tensor(yout[:, t % 2, :], yout[:, t % 2, :], xre[:, t % 2, :], ALU.add)\
                    .then_inc(s["v_y"], 1)

            parts = {"prep": prep, "xT": xT, "angles": angles, "evac": evac, "score": score, "topk": topk, "gz": gz,
                     "logalpha": logalpha, "qkdiag": qkdiag, "qinter": qinter, "level": level, "pairs": pairs,
                     "kv": kv, "glaout": glaout, "glafin": glafin, "qk": qk_, "pT": pT, "attfin": attfin,
                     "wprep": wprep, "mixT": mixT, "fin": fin}
            for step in plan:
                if step[0] in parts:
                    parts[step[0]](*step[1:])

        @block.gpsimd
        def _(pool):
            G = nc.gpsimd
            G.memset(idxrow[:, :, IW0 + IDX_HEADS:], 0.0).then_inc(s["g_init"], 1)
            G.memset(pwr[:, :], -0.5).then_inc(s["g_init"], 1)
            pool.wait_ge(d_mask, 16)
            G.tensor_copy(lvl[:, :, :], lvl_in[:, :, :]).then_inc(s["g_init"], 1)
            pool.wait_ge(s["g_init"], 3)
            G.memset(AT[:, :, :, :], 0.0).then_inc(s["g_init"], 1)
            pool.wait_ge(s["g_init"], 4)
            roped = [0]

            def ssq_(t):
                if t < TILES - 1:
                    return
                pool.wait_ge(s["a_ssq"], TILES)
                G.tensor_scalar(ssq[:, 1, :], ssq[:, 0, :], 1 / D_MODEL, EPS, ALU.mult, ALU.add)\
                    .then_inc(s["g_rstd"], 1)
                pool.wait_ge(s["g_rstd"], 1)
                G.tensor_tensor(ssq[:, 2, :], ssq[:, 1, :], pwr[:, :].broadcast_to([P, TILES]), ALU.pow)\
                    .then_inc(s["g_rstd"], 1)
                pool.wait_ge(s["g_rstd"], 2)
                G.tensor_scalar(ssq[:, 3, :], ssq[:, 2, :], 0.5, None, ALU.mult).then_inc(s["g_rstd"], 1)

            def rope(a, t):
                heads = a.shape[1]
                x4 = a[:, :, 0:2 * HALF]
                by_cos, by_sin = (ropet[:, n, 0:heads, :] for n in range(2))
                over = [P, heads, HALF]
                if roped[0] > 0:
                    pool.wait_ge(s["g_rope"], roped[0])
                else:
                    pool.wait_ge(s["a_ang"], 4)
                roped[0] += 1
                G.tensor_tensor(by_cos, x4, cosd[:, t, :, :].rearrange("p a b -> p (a b)").unsqueeze(1)
                                .broadcast_to([P, heads, 2 * HALF]), ALU.mult).then_inc(s["g_ropet"], 1)
                for n in range(2):
                    G.tensor_tensor(by_sin[:, :, HALF * n:HALF * (n + 1)], x4[:, :, HALF * (1 - n):HALF * (2 - n)],
                                    sind[:, t, n, :].unsqueeze(1).broadcast_to(over), ALU.mult)\
                        .then_inc(s["g_ropet"], 1)
                pool.wait_ge(s["g_ropet"], 3 * roped[0])
                return G.tensor_tensor(x4, by_cos, by_sin, ALU.add)

            def evac(c, t):
                if c == C_IDX:
                    wait_moved(pool, ("proj", c, t))
                    rope(idxrow[:, t, 0:320].rearrange("p (h n) -> p h n", h=5), t).then_inc(s["g_iw"], 1)
                    G.tensor_scalar(iw[:, t, :], idxrow[:, t, IW0:IW0 + IDX_HEADS], (IDX_HEADS * IDX_HD) ** -0.5, None,
                                    ALU.mult).then_inc(s["g_iw"], 1)
                    pool.wait_ge(s["g_iw"], 2 * (t + 1))
                    G.tensor_copy(idxrow[:, t, 320:384], idxrow[:, t, 256:320]).then_inc(s["g_rope"], 1)
                elif c in (C_AQ, C_AK):
                    wait_moved(pool, ("proj", c, t))
                    rope(row[:, t, :].rearrange("p (h n) -> p h n", h=ATT_HEADS), t).then_inc(s["g_rope"], 1)
                elif c == C_GGATE:
                    pool.wait_ge(s["v_gate"], TILES + t + 1)
                    if t == 0:
                        pool.wait_ge(d_small, 48)
                    g = xm[:, t, ATT_W:].rearrange("p (h n) -> p h n", h=GLA_HEADS)
                    G.tensor_tensor(g, g, glaw[:, :].unsqueeze(1).broadcast_to([P, GLA_HEADS, GLA_DV]), ALU.mult)\
                        .then_inc(s["g_gate"], 1)

            def level(lev):
                if lev > 0:
                    return
                pool.wait_ge(s["v_qk"], 3)
                for t in range(TILES - 1):
                    wait_moved(pool, ("rowT", C_GQK, t))
                    wait_moved(pool, ("cum", t))
                    k = grow[:, t, 256:512]
                    G.tensor_tensor(k, k, lg[:, t, :], ALU.mult).then_inc(s["g_kt"], 1)

            def glaout(t):
                n = GLA_HEADS * t
                pool.wait_ge(s["a_gsq"], n + GLA_HEADS)
                G.tensor_scalar(gss[:, 1, n:n + 4], gss[:, 0, n:n + 4], 1 / GLA_DV, EPS, ALU.mult, ALU.add)\
                    .then_inc(s["g_grs"], 1)
                pool.wait_ge(s["g_grs"], 2 * t + 1)
                G.tensor_tensor(gss[:, 2, n:n + 4], gss[:, 1, n:n + 4], pwr[:, :].broadcast_to([P, 4]), ALU.pow)\
                    .then_inc(s["g_grs"], 1)

            def outp(t):
                pool.wait_ge(s["a_osq"], 2 * (t + 1))
                c = slice(t, t + 1)
                G.tensor_tensor(oss[:, 2, c], oss[:, 0, c], oss[:, 1, c], ALU.add).then_inc(s["g_ors"], 1)
                pool.wait_ge(s["g_ors"], 3 * t + 1)
                G.tensor_scalar(oss[:, 3, c], oss[:, 2, c], 1 / D_MODEL, EPS, ALU.mult, ALU.add)\
                    .then_inc(s["g_ors"], 1)
                pool.wait_ge(s["g_ors"], 3 * t + 2)
                G.tensor_tensor(oss[:, 4, c], oss[:, 3, c], pwr[:, :], ALU.pow).then_inc(s["g_ors"], 1)

            parts = {"ssq": ssq_, "evac": evac, "level": level, "glaout": glaout, "outp": outp}
            for step in plan:
                if step[0] in parts:
                    parts[step[0]](*step[1:])


def kernel(**inputs):
    import numpy as np
    import concourse.bacc as bacc
    from concourse.bass_utils import run_bass_kernel_spmd as run

    nc = bacc.Bacc("TRN2", target_bir_lowering=False, num_devices=1)
    i = np.arange(P)
    consts = np.zeros((P, NCONST), np.float32)
    consts[:, IDENT:IDENT + P] = np.eye(P)
    consts[:, CUM:CUM + P] = i[:, None] <= i[None, :]
    consts[:, REV:REV + P] = i[:, None] > i[None, :]
    consts[:, CAUSAL:CAUSAL + P] = np.where(i[None, :] <= i[:, None], 0.0, NEG)
    freq = np.float32(500000.0) ** (-np.arange(0, 2 * HALF, 2, dtype=np.float32) / np.float32(2 * HALF))
    consts[:, FREQ:FREQ + HALF] = freq
    far = i[:, None] ^ i[None, :]
    masks = np.stack([(far >> (LEVELS - 1 - lev) == 1) & (i[None, :] > i[:, None]) for lev in range(LEVELS)], 1)
    arrays, aps = {}, []
    for name in ("x", "positions", "w_in", "w_gla_gate_up", "b_gla_gate", "gla_norm_w", "w_out", "pre_norm_w",
                 "post_norm_w"):
        arrays["in_" + name] = np.ascontiguousarray(inputs[name])
    arrays["in_positions"] = np.ascontiguousarray(arrays["in_positions"].reshape(TILES, P).T)
    arrays["in_consts"] = consts
    arrays["in_masks"] = masks.astype(np.int32)
    for name, a in arrays.items():
        aps.append(nc.dram_tensor(name, a.shape, mybir.dt.from_np(a.dtype), kind="ExternalInput").ap())
    out = nc.dram_tensor("out", (1, SEQ, D_MODEL), F32, kind="ExternalOutput").ap()
    layer_kernel(nc, *aps, out)
    return run(nc, [arrays], core_ids=[0]).results[0]["out"]
```

```python
from contextlib import ExitStack

import concourse.bass as bass
from concourse import mybir

P = 128
SEQ, D_MODEL = 512, 1024
TILES = SEQ // P
KT = D_MODEL // P
ATT_HEADS, ATT_HD = 8, 64
IDX_HEADS, IDX_HD = 4, 64
GLA_HEADS, GLA_DK, GLA_DV, GATE_RANK = 4, 64, 128, 16
ATT_W, GLA_W = ATT_HEADS * ATT_HD, GLA_HEADS * GLA_DV
HALF = ATT_HD // 4 // 2
KSEL = SEQ // 4
ROUNDS = KSEL // 8
EPS = 1e-6
NEG = -1e30
TAKEN = -3e38
LEVELS = 7
PI = 3.141592653589793
PI_BELOW = 3.1415925
TWO_PI = (6.28125, 0.0019350051879882812, 3.0199159819e-07)

F32 = mybir.dt.float32
F32R = mybir.dt.float32r
I32 = mybir.dt.int32
U8 = mybir.dt.uint8
ALU = mybir.AluOpType
ACT = mybir.ActivationFunctionType
AX = mybir.AxisListType

CHUNKS = [
    [(1536, 324), (3396, 16)],
    [(2372, 512)],
    [(0, 512)],
    [(512, 512)],
    [(1024, 512)],
    [(1860, 512)],
    [(2884, 512)],
    [(3412, 512)],
]
C_IDX, C_GQK, C_AQ, C_AK, C_AV, C_AGATE, C_GV, C_GGATE = range(8)
NC = len(CHUNKS)
WIDTH = [sum(w for _, w in c) for c in CHUNKS]
WOUT_PIECES = 4
LR0, IW0 = 384, 400
IDENT, CUM, REV, CAUSAL, FREQ, NCONST = 0, 128, 256, 384, 512, 520

GENERAL = [4, 5, 6]
GENERAL_LATE = [4, 5, 6, 0, 1]
OUT_BANKS = [2, 3]
O_BANK = 7


def pT_on_act(u):
    return u % 2 == 0


def units(tiles):
    return [(t, h) for t in tiles for h in range(ATT_HEADS)]


def schedule():
    groups = [(c, half, t) for c in range(NC) for half in range(2) for t in range(TILES)]
    fill = {g: [] for g in groups}

    def at(c, half, t, *steps):
        fill[(c, half, t)].extend(steps)

    for t in range(TILES):
        at(C_IDX + 1, 0, t // 2, ("idxT", t))
        at(C_IDX + 1, 1, t // 2, ("gz", t))
        at(C_GQK + 1, 0, t, ("rowT", C_GQK, t), ("cum", t))
        at(C_AQ + 1, 0, t, ("rowT", C_AQ, t))
        at(C_AK + 1, 0, t, ("rowT", C_AK, t))
        at(C_GV + 1, 0, t, ("kv", t))
    for t in range(1, TILES):
        at(*groups[groups.index((C_IDX + 1, 0, 1)) + t], *[("score", t, h) for h in range(IDX_HEADS)])
    at(C_IDX + 1, 1, 2, ("logalpha",))
    at(C_GQK + 1, 0, 0, ("qkdiag",))
    at(C_GQK + 1, 0, 3, ("qinter",), ("level", 0))
    first = groups.index((C_IDX + 1, 1, 1))
    rounds = [("topk", t, r) for t in range(1, TILES) for r in range(ROUNDS)]
    for n, step in enumerate(rounds):
        at(*groups[first + n], step)
    first, last = groups.index((C_GQK + 1, 1, 1)), groups.index((C_GV, 0, 3))
    for n in range(2 * LEVELS):
        lev, odd = divmod(n, 2)
        g = first + n * (last - first) // (2 * LEVELS - 1)
        if odd == 0 and lev > 0:
            at(*groups[g - 2], ("level", lev))
        at(*groups[g], ("pairs", lev, odd))
    first = groups.index((C_AV + 1, 0, 0))
    for n, u in enumerate(units(range(TILES - 1))):
        at(*groups[first + n], ("unit", *u))
    for t in range(2):
        at(NC - 1, 1, t + 1, ("glaout", t))
        at(NC - 1, 1, t + 2, ("glafin", t))

    at(NC - 1, 1, 0, ("wprep", 0))
    at(NC - 1, 1, 2, ("wprep", 1))

    plan = [("xT", 0, 0), ("xT", 0, 1), ("prep", 0), ("xT", 1, 0), ("ssq", 0), ("xT", 1, 1)]
    for c, half, t in groups:
        plan.append(("proj", c, half, t))
        n = 2 * c + half
        if n == 0:
            plan += [[("xT", 2, 0), ("prep", 1), ("ssq", 1), ("xT", 2, 1)], [("xT", 3, 0), ("ssq", 2), ("xT", 3, 1)],
                     [("angles",), ("ssq", 3)], [("masks",)]][t]
        elif t == 0 and n < 2 * NC - 1:
            plan.append(("prep", n + 1))
        if half == 1:
            plan.append(("evac", c, t))
        plan += fill[(c, half, t)]
    between = [[("glaout", 2), ("wprep", 2)], [("wprep", 3), ("glafin", 2)], [("glaout", 3), ("mixT", 0, 0), ("mixT", 0, 1)],
               [("glafin", 3), ("mixT", 1, 0), ("mixT", 1, 1)], [("mixT", 2, 0), ("mixT", 2, 1)], [("outp", 0, 0)],
               [("outp", 0, 1), ("fin", 0)], [("outp", 1, 0)]]
    for u, steps in zip(units([TILES - 1]), between):
        plan.append(("unit", *u))
        plan += steps
    plan += [("behind",), ("outp", 1, 1), ("fin", 1), ("behind",), ("outp", 2, 0), ("mixT", 3, 0), ("mixT", 3, 1),
             ("outp", 2, 1), ("fin", 2), ("outp", 3, 0), ("outp", 3, 1), ("fin", 3)]

    out, all_units, n = [], units(range(TILES)), 0
    for step in plan:
        if step[0] not in ("unit", "behind"):
            out.append(step)
            continue
        if step[0] == "unit":
            out.append(("qk", *step[1:]))
        if 0 < n <= len(all_units):
            out.append(("pT", *all_units[n - 1]))
        if n > 1:
            out.append(("pv", *all_units[n - 2]))
            if all_units[n - 2][1] == ATT_HEADS - 1:
                out.append(("attfin", all_units[n - 2][0]))
        n += 1
    return out


def psum_jobs(plan):
    jobs, used, ring = {}, [0] * 8, 0

    def take(key, bank):
        jobs[key] = (bank, used[bank])
        used[bank] += 1

    late = False
    for s in plan:
        if s[0] == "proj" and s[2] == 0:
            take(("proj", s[1], s[3]), s[3])
        elif s[0] in ("xT", "idxT", "score", "gz", "rowT", "cum", "pairs", "kv", "qk", "pT", "mixT"):
            if s[0] == "kv" and s[1] == TILES - 1:
                continue
            banks = GENERAL_LATE if late else GENERAL
            take(s, banks[ring % len(banks)])
            ring += 1
        elif s[0] == "glaout":
            banks = GENERAL_LATE if late else GENERAL
            for odd in range(2):
                take((*s, odd), banks[ring % len(banks)])
                ring += 1
        elif s[0] == "pv" and s[2] == 0:
            take(("att", s[1]), O_BANK)
        elif s[0] == "outp":
            take(s, OUT_BANKS[s[2]])
        if s == ("proj", NC - 1, 1, TILES - 1):
            late = True
    return jobs


def layer_kernel(nc, x, positions, w_in, w_up, b_gate, gla_norm_w, w_out, pre_norm_w, post_norm_w,
                 consts, level_masks, out):
    plan = schedule()
    jobs = psum_jobs(plan)
    UNITS = [s[1:] for s in plan if s[0] == "qk"]
    unit_no = {u: n for n, u in enumerate(UNITS)}
    PAIRS = [s[1:] for s in plan if s[0] == "pairs"]
    x_v = x.rearrange("b (t p) d -> (b t) p d", p=P)
    out_v = out.rearrange("b (t p) d -> (b t) p d", p=P)
    w_in_v = w_in.rearrange("(p k) n -> p k n", k=KT)
    w_out_v = w_out.rearrange("(p k) n -> p k n", k=KT)

    with ExitStack() as ctx:
        place = [(nc.sbuf_base + 63) // 32 * 32]

        def put(name, shape, dt=F32, offset=None):
            size = {F32: 4, F32R: 4, I32: 4, U8: 1}[dt]
            for n in shape[1:]:
                size *= n
            at = place[0] if offset is None else offset
            if offset is None:
                place[0] += (size + 31) // 32 * 32
            return nc.alloc_sbuf_tensor_at(name, shape, dt, offset=at), at

        def sb(name, shape, dt=F32, offset=None):
            return put(name, shape, dt, offset)[0]

        def sem(name):
            return ctx.enter_context(nc.semaphore(name))

        cst = sb("cst", [P, NCONST])
        lvl = sb("lvl", [P, LEVELS, P], U8)
        prew = sb("prew", [P, KT])
        glaw = sb("glaw", [P, GLA_DV])
        bgate = sb("bgate", [P, GLA_HEADS * GLA_DK])
        wup = sb("wup", [GATE_RANK, GLA_HEADS * GLA_DK])
        pos = sb("pos", [P, TILES], I32)
        ang = sb("ang", [P, 4, TILES, HALF])
        cosd = sb("cosd", [P, TILES, 2, HALF])
        sind = sb("sind", [P, TILES, 2, HALF])
        ropet = sb("ropet", [P, 2, ATT_HEADS, 2 * HALF])
        ssq = sb("ssq", [P, 4, TILES])
        iw = sb("iw", [P, TILES, IDX_HEADS])
        best = sb("best", [P, 8])
        nmax = sb("nmax", [P, TILES * ATT_HEADS])
        psums = sb("psums", [P, TILES * ATT_HEADS])
        rinv = sb("rinv", [P, TILES * ATT_HEADS])
        qkd = sb("qkd", [P, 2, TILES * GLA_HEADS])
        dec = sb("dec", [P, 2, TILES])
        gss = sb("gss", [P, 3, TILES * GLA_HEADS])
        oss = sb("oss", [P, 5, TILES])
        pwr = sb("pwr", [P, 1])
        xm = sb("xm", [P, TILES, D_MODEL])
        hT_hi = sb("hT_hi", [P, KT, SEQ], F32R)
        hT_lo = sb("hT_lo", [P, KT, SEQ], F32R)
        w_hi = sb("w_hi", [P, 2, KT // 2, 512], F32R)
        w_lo = sb("w_lo", [P, 2, KT // 2, 512], F32R)
        raw = sb("raw", [P, 2, KT // 2, 512])
        aqT = sb("aqT", [P, 4, SEQ])
        akT = sb("akT", [P, 4, SEQ])
        av = sb("av", [P, TILES, ATT_W])
        row, row_at = put("row", [P, TILES, 512])
        idxrow, idx_at = put("idxrow", [P, TILES, 512])
        idxT = sb("idxT", [P, 4, SEQ])
        gqkT = sb("gqkT", [P, 4, SEQ], offset=idx_at)
        bT = sb("bT", [P, 2, SEQ], offset=idx_at + 8192)
        qi = sb("qi", [P, 2, SEQ], offset=idx_at + 12288)
        yout = sb("yout", [P, 2, D_MODEL], offset=idx_at)
        xre = sb("xre", [P, 2, D_MODEL], offset=idx_at + 8192)
        work, work_at = put("work", [P, 1152])
        postw = sb("postw", [P, D_MODEL], offset=work_at)
        bias = sb("bias", [P, 1280])
        grow, grow_at = put("grow", [P, TILES, 512])
        gv, gv_at = put("gv", [P, TILES, GLA_W])
        X = sb("X", [P, 2, 2, SEQ], offset=gv_at)
        lg, lg_at = put("lg", [P, TILES, 256])
        og = sb("og", [P, 2, 512], offset=lg_at)
        Pb, p_at = put("Pb", [P, 2, 512])
        lgt = sb("lgt", [P, TILES, 256], offset=p_at)
        pTb, pt_at = put("pTb", [P, 2, 512])
        rel = sb("rel", [P, 2, 512], offset=pt_at)
        E = sb("E", [P, 2, SEQ])
        AT, at_at = put("AT", [P, GLA_HEADS, TILES, P])
        lvl_in = sb("lvl_in", [P, LEVELS, P], I32, offset=at_at)
        mT_hi, mT_lo = ([sb(f"mT_{part}{t}", [P, KT, P], F32R, offset=at + 4 * P * KT * n)
                         for t, (at, n) in enumerate(places)] for part, places in (
            ("hi", [(row_at, 0), (row_at, 1), (at_at, 0), (gv_at, 0)]),
            ("lo", [(grow_at, 0), (grow_at, 1), (at_at, 1), (gv_at, 1)])))
        S = sb("S", [P, TILES - 1, 2, GLA_DV])
        th = sb("th", [P, 512])
        assert place[0] <= nc.sbuf_usable_end, place[0] - nc.sbuf_usable_end

        bank = [ctx.enter_context(nc.psum_tensor(f"bank{n}", [P, 512], F32)) for n in range(8)]
        full = [sem(f"bank{n}_full") for n in range(8)]
        moved = [sem(f"bank{n}_moved") for n in range(8)]

        d_ident, d_cst, d_prew, d_small, d_mask, d_pos, d_post = (sem(n) for n in (
            "d_ident", "d_cst", "d_prew", "d_small", "d_mask", "d_pos", "d_post"))
        d_x = [sem(f"d_x{t}") for t in range(TILES)]
        d_raw = [sem(f"d_raw{n}") for n in range(2)]
        d_xre = [sem(f"d_xre{n}") for n in range(2)]
        d_out = [sem(f"d_out{n}") for n in range(2)]
        names = ("a_ssq a_hTh a_whi a_ang a_th a_la a_dec a_E a_p a_gsq a_mTh a_osq a_wo "
                 "g_hTl v_wlo v_ang v_score v_cand v_best v_bias v_lg v_gate v_qk v_qi v_D v_X "
                 "v_gm v_rinv v_am v_mean v_y v_wo "
                 "g_init g_rstd g_ropet g_rope g_iw g_kt g_gate g_grs g_ors t_half t_pv").split()
        s = {n: sem(n) for n in names}

        def raw_value(n):
            pieces = [len(CHUNKS[m // 2]) if m < 2 * NC else 1 for m in range(n % 2, n + 1, 2)]
            return 16 * sum(pieces)

        def wait_full(eng, key):
            b, n = jobs[key]
            eng.wait_ge(full[b], n + 1)
            return bank[b]

        def is_free(eng, key):
            b, n = jobs[key]
            if n > 0:
                eng.wait_ge(moved[b], n)
            return bank[b]

        def wait_moved(eng, key):
            b, n = jobs[key]
            eng.wait_ge(moved[b], n + 1)

        def half_done(eng, n):
            c, half = divmod(n, 2)
            if half == 0:
                eng.wait_ge(s["t_half"], c + 1)
            else:
                wait_full(eng, ("proj", c, TILES - 1))

        def pv_done(eng, n):
            t, h = UNITS[n]
            if h == ATT_HEADS - 1:
                wait_full(eng, ("att", t))
            else:
                eng.wait_ge(s["t_pv"], n - t)

        def filled(key):
            return full[jobs[key][0]]

        def emptied(key):
            return moved[jobs[key][0]]

        def ident():
            return cst[:, IDENT:IDENT + P]

        block = ctx.enter_context(nc.Block())

        @block.sync
        def _(sp):
            def load_weights(n):
                if n >= 2:
                    if n - 2 < 2 * NC:
                        sp.wait_ge(s["a_whi"], n - 1)
                        sp.wait_ge(s["v_wlo"], n - 1)
                    else:
                        sp.wait_ge(s["a_wo"], 2 * (n - 1 - 2 * NC))
                        sp.wait_ge(s["v_wo"], 2 * (n - 1 - 2 * NC))
                if n < 2 * NC:
                    c, half = divmod(n, 2)
                    col = 0
                    for first, width in CHUNKS[c]:
                        sp.dma_start(raw[:, n % 2, :, col:col + width],
                                     w_in_v[:, half * KT // 2:(half + 1) * KT // 2, first:first + width]
                                     ).then_inc(d_raw[n % 2], 16)
                        col += width
                else:
                    j = n - 2 * NC
                    sp.dma_start(raw[:, n % 2, :, :].rearrange("p k n -> p (k n)"),
                                 w_out_v[:, 2 * j:2 * j + 2, :].rearrange("p k n -> p (k n)")
                                 ).then_inc(d_raw[n % 2], 16)

            sp.dma_start(xm[:, 0, :], x_v[0]).then_inc(d_x[0], 16)
            sp.dma_start(cst[:, 0:P], consts[:, 0:P]).then_inc(d_ident, 16)
            load_weights(0)
            for t in range(1, TILES):
                sp.dma_start(xm[:, t, :], x_v[t]).then_inc(d_x[t], 16)
            load_weights(1)
            sp.dma_start(cst[:, P:], consts[:, P:]).then_inc(d_cst, 16)
            sp.dma_start(lvl_in[:, :, :], level_masks).then_inc(d_mask, 16)
            for n in range(2, 2 * NC + WOUT_PIECES):
                load_weights(n)
            sp.wait_ge(s["v_bias"], TILES - 1)
            sp.dma_start(postw[:, :], post_norm_w.partition_broadcast(P)).then_inc(d_post, 16)
            wait_moved(sp, ("glaout", TILES - 1, 1))
            for t in range(2):
                sp.dma_start(xre[:, t % 2, :], x_v[t]).then_inc(d_xre[t % 2], 16)
            for t in range(TILES):
                for n in range(2):
                    cols = slice(512 * n, 512 * (n + 1))
                    sp.wait_ge(s["v_y"], 2 * t + n + 1)
                    sp.dma_start(out_v[t][:, cols], yout[:, t % 2, cols]).then_inc(d_out[t % 2], 16)
                if t + 2 < TILES:
                    sp.dma_start(xre[:, t % 2, :], x_v[t + 2]).then_inc(d_xre[t % 2], 16)
            for n in range(2):
                sp.wait_ge(d_out[n], 16 * TILES)

        @block.tensor
        def _(pe):
            def xT(t, g):
                if g == 0:
                    pe.wait_ge(d_x[t], 16)
                    if t == 0:
                        pe.wait_ge(d_ident, 16)
                b = is_free(pe, ("xT", t, g))
                for j in range(4):
                    k = 4 * g + j
                    last = nc.tensor.transpose(b[:, P * j:P * (j + 1)], xm[:, t, k::KT], ident())
                last.then_inc(filled(("xT", t, g)), 1)

            def proj(c, half, t):
                n, w = 2 * c + half, WIDTH[c]
                b = bank[t]
                if t == 0:
                    pe.wait_ge(s["a_whi"], n + 1)
                    pe.wait_ge(s["v_wlo"], n + 1)
                if n == 0:
                    pe.wait_ge(s["g_hTl"], 2 * (t + 1))
                if half == 0:
                    is_free(pe, ("proj", c, t))
                for j in range(KT // 2):
                    k = half * (KT // 2) + j
                    h_hi, h_lo = (a[:, k, P * t:P * (t + 1)] for a in (hT_hi, hT_lo))
                    v_hi, v_lo = (a[:, n % 2, j, 0:w] for a in (w_hi, w_lo))
                    nc.tensor.matmul(b[:, 0:w], h_hi, v_hi, start=(k == 0), stop=False)
                    nc.tensor.matmul(b[:, 0:w], h_hi, v_lo, start=False, stop=False)
                    last = nc.tensor.matmul(b[:, 0:w], h_lo, v_hi, start=False, stop=(k == KT - 1))
                if half == 1:
                    last.then_inc(full[t], 1)
                if half == 0 and t == TILES - 1:
                    last.then_inc(s["t_half"], 1)

            def idxT_(t):
                pe.wait_ge(s["g_rope"], t + 1)
                b = is_free(pe, ("idxT", t))
                for j in range(4):
                    last = nc.tensor.transpose(b[:, P * j:P * (j + 1)], idxrow[:, t, P * j:P * (j + 1)], ident())
                last.then_inc(filled(("idxT", t)), 1)

            def score(t, h):
                n = (t + 1) * P
                if h == 0:
                    wait_moved(pe, ("idxT", t))
                b = is_free(pe, ("score", t, h))
                lo = 64 * (h % 2)
                nc.tensor.matmul(b[:, 0:n], idxT[lo:lo + 64, h // 2, P * t:P * (t + 1)], idxT[lo:lo + 64, 2, 0:n],
                                 start=True, stop=True).then_inc(filled(("score", t, h)), 1)

            def gz(t):
                wait_moved(pe, ("idxT", t))
                if t == 0:
                    pe.wait_ge(d_small, 48)
                b = is_free(pe, ("gz", t))
                nc.tensor.matmul(b[:, 0:256], idxT[0:GATE_RANK, 3, P * t:P * (t + 1)], wup[:, :],
                                 start=True, stop=True).then_inc(filled(("gz", t)), 1)

            def rowT(c, t):
                src = row if c != C_GQK else grow
                if c == C_GQK:
                    wait_moved(pe, ("proj", c, t))
                else:
                    pe.wait_ge(s["g_rope"], TILES * (1 + (C_AQ, C_AK).index(c)) + t + 1)
                b = is_free(pe, ("rowT", c, t))
                for j in range(4):
                    last = nc.tensor.transpose(b[:, P * j:P * (j + 1)], src[:, t, P * j:P * (j + 1)], ident())
                last.then_inc(filled(("rowT", c, t)), 1)

            def cum(t):
                pe.wait_ge(s["v_lg"], 1)
                pe.wait_ge(d_cst, 16)
                b = is_free(pe, ("cum", t))
                for g in range(2):
                    nc.tensor.matmul(b[:, P * g:P * (g + 1)], lg[:, t, P * g:P * (g + 1)], cst[:, CUM:CUM + P],
                                     start=True, stop=True)
                nc.tensor.matmul(b[:, 256:512], cst[:, REV:REV + P], lg[:, t, :],
                                 start=True, stop=True).then_inc(filled(("cum", t)), 1)

            def pairs(lev, odd):
                key = ("pairs", lev, odd)
                pe.wait_ge(s["v_X"], 2 * (lev + 1))
                b = is_free(pe, key)
                for n in range(GLA_HEADS // 2 * TILES):
                    g, t = divmod(n, TILES)
                    x = X[64 * odd:64 * odd + 64, lev % 2, g, P * t:P * (t + 1)]
                    for part in range(1 if lev == 0 else 2):
                        a, c = (0, 64) if lev == 0 else (64 * part, 64 * part)
                        last = nc.tensor.matmul(b[64 * part:64 * part + 64, 64 * n:64 * (n + 1)],
                                                x[:, a:a + 64], x[:, c:c + 64], start=True, stop=True)
                last.then_inc(filled(key), 1)

            def kv(t):
                if t == TILES - 1:
                    return
                pe.wait_ge(s["g_kt"], t + 1)
                wait_moved(pe, ("proj", C_GV, t))
                b = is_free(pe, ("kv", t))
                for h in range(GLA_HEADS):
                    lo = 64 * (h % 2)
                    last = nc.tensor.matmul(b[lo:lo + 64, P * (h // 2):P * (h // 2 + 1)],
                                            grow[:, t, 256 + 64 * h:256 + 64 * (h + 1)],
                                            gv[:, t, P * h:P * (h + 1)], start=True, stop=True)
                last.then_inc(filled(("kv", t)), 1)

            def glaout(t):
                for lev in (0, LEVELS - 1):
                    for odd in range(2):
                        wait_moved(pe, ("pairs", lev, odd))
                pe.wait_ge(s["v_qi"], 1)
                if t > 0:
                    wait_moved(pe, ("kv", t - 1))
                for odd in range(2):
                    key = ("glaout", t, odd)
                    b = is_free(pe, key)
                    for h in range(odd, GLA_HEADS, 2):
                        lo, o = 64 * odd, b[:, P * (h // 2):P * (h // 2 + 1)]
                        last = nc.tensor.matmul(o, AT[:, h, t, :], gv[:, t, P * h:P * (h + 1)],
                                                start=True, stop=(t == 0))
                        if t > 0:
                            last = nc.tensor.matmul(o, qi[lo:lo + 64, h // 2, P * t:P * (t + 1)],
                                                    S[lo:lo + 64, t - 1, h // 2, :], start=False, stop=True)
                    last.then_inc(filled(key), 1)

            def qk_(t, h):
                n, lo = (t + 1) * P, 64 * (h % 2)
                if h == 0:
                    wait_moved(pe, ("rowT", C_AK, TILES - 1))
                b = is_free(pe, ("qk", t, h))
                nc.tensor.matmul(b[:, 0:n], aqT[lo:lo + 64, h // 2, P * t:P * (t + 1)], akT[lo:lo + 64, h // 2, 0:n],
                                 start=True, stop=True).then_inc(filled(("qk", t, h)), 1)

            def pT(t, h):
                u = unit_no[(t, h)]
                pe.wait_ge(s["a_p"], u + 1)
                b = is_free(pe, ("pT", t, h))
                for j in range(t + 1):
                    last = nc.tensor.transpose(b[:, P * j:P * (j + 1)], Pb[:, u % 2, P * j:P * (j + 1)], ident())
                last.then_inc(filled(("pT", t, h)), 1)

            def pv(t, h):
                u = unit_no[(t, h)]
                wait_moved(pe, ("pT", t, h))
                if h == 0:
                    wait_moved(pe, ("proj", C_AV, t))
                    is_free(pe, ("att", t))
                b = bank[O_BANK]
                for j in range(t + 1):
                    last = nc.tensor.matmul(b[:, 64 * h:64 * (h + 1)], pTb[:, u % 2, P * j:P * (j + 1)],
                                            av[:, j, 64 * h:64 * (h + 1)], start=(j == 0), stop=(j == t))
                if h == ATT_HEADS - 1:
                    last.then_inc(full[O_BANK], 1)
                else:
                    last.then_inc(s["t_pv"], 1)

            def mixT(t, g):
                pe.wait_ge(s["v_am"], t + 1)
                pe.wait_ge(s["v_gm"], GLA_HEADS * (t + 1))
                b = is_free(pe, ("mixT", t, g))
                for j in range(4):
                    last = nc.tensor.transpose(b[:, P * j:P * (j + 1)], xm[:, t, 4 * g + j::KT], ident())
                last.then_inc(filled(("mixT", t, g)), 1)

            def outp(t, n):
                key = ("outp", t, n)
                if t == 0 and n == 0:
                    pe.wait_ge(s["a_wo"], 2 * WOUT_PIECES)
                    pe.wait_ge(s["v_wo"], 2 * WOUT_PIECES)
                if n == 0:
                    wait_moved(pe, ("mixT", t, 0))
                    wait_moved(pe, ("mixT", t, 1))
                b = is_free(pe, key)
                for k in range(KT):
                    m_hi, m_lo = mT_hi[t][:, k, :], mT_lo[t][:, k, :]
                    if n == 0:
                        v_hi, v_lo = hT_hi[:, k, :], hT_lo[:, k, :]
                    else:
                        v_hi, v_lo = (a[:, k // 4, k % 4, :] for a in (w_hi, w_lo))
                    nc.tensor.matmul(b[:, :], m_hi, v_hi, start=(k == 0), stop=False)
                    nc.tensor.matmul(b[:, :], m_hi, v_lo, start=False, stop=False)
                    last = nc.tensor.matmul(b[:, :], m_lo, v_hi, start=False, stop=(k == KT - 1))
                last.then_inc(filled(key), 1)

            parts = {"xT": xT, "proj": proj, "idxT": idxT_, "score": score, "gz": gz, "rowT": rowT, "cum": cum,
                     "pairs": pairs, "kv": kv, "glaout": glaout, "qk": qk_, "pT": pT, "pv": pv, "mixT": mixT,
                     "outp": outp}
            for step in plan:
                if step[0] in parts:
                    parts[step[0]](*step[1:])

        @block.scalar
        def _(act):
            act.dma_start(prew[:, :], pre_norm_w.rearrange("(p k) -> p k", k=KT)).then_inc(d_prew, 16)
            act.dma_start(pos[:, :], positions).then_inc(d_pos, 16)
            act.dma_start(wup[:, :], w_up).then_inc(d_small, 16)
            act.dma_start(bgate[:, :], b_gate.partition_broadcast(P)).then_inc(d_small, 16)
            act.dma_start(glaw[:, :], gla_norm_w.partition_broadcast(P)).then_inc(d_small, 16)
            def angles():
                act.wait_ge(s["v_ang"], 9)
                nc.scalar.activation(sind[:, :, 1, :], ang[:, 2, :, :], ACT.Sin).then_inc(s["a_ang"], 1)
                nc.scalar.activation(cosd[:, :, 0, :], ang[:, 3, :, :], ACT.Sin).then_inc(s["a_ang"], 1)
                act.wait_ge(s["a_ang"], 2)
                nc.scalar.activation(sind[:, :, 0, :], sind[:, :, 1, :], ACT.Copy, scale=-1.0).then_inc(s["a_ang"], 1)
                nc.scalar.activation(cosd[:, :, 1, :], cosd[:, :, 0, :], ACT.Copy).then_inc(s["a_ang"], 1)

            def prep(n):
                w = WIDTH[n // 2]
                act.wait_ge(d_raw[n % 2], raw_value(n))
                if n >= 2:
                    half_done(act, n - 2)
                nc.scalar.activation(w_hi[:, n % 2, :, 0:w], raw[:, n % 2, :, 0:w], ACT.Copy).then_inc(s["a_whi"], 1)

            def xT(t, g):
                j = 2 * t + g
                wait_moved(act, ("xT", t, g))
                nc.scalar.activation(hT_hi[:, 4 * g:4 * g + 4, P * t:P * (t + 1)],
                                     row[:, j % 4, :].rearrange("p (k n) -> p k n", k=4),
                                     ACT.Copy).then_inc(s["a_hTh"], 1)

            def ssq_(t):
                act.wait_ge(d_x[t], 16)
                if t > 0:
                    act.wait_ge(s["a_ssq"], t)
                nc.scalar.activation(E[:, :, :].rearrange("p a b -> p (a b)"), xm[:, t, :], ACT.Square,
                                     accum_out=ssq[:, 0, t:t + 1]).then_inc(s["a_ssq"], 1)

            def evac(c, t):
                key = ("proj", c, t)
                b = wait_full(act, key)
                rstd, hrstd = ssq[:, 2, t:t + 1], ssq[:, 3, t:t + 1]
                act.wait_ge(s["g_rstd"], 3)
                if c == C_IDX:
                    nc.scalar.activation(idxrow[:, t, 0:320], b[:, 0:320], ACT.Copy, scale=rstd)
                    nc.scalar.activation(idxrow[:, t, IW0:IW0 + 4], b[:, 320:324], ACT.Copy, scale=rstd)
                    nc.scalar.activation(idxrow[:, t, LR0:LR0 + GATE_RANK], b[:, 324:340], ACT.Copy, scale=rstd)\
                        .then_inc(emptied(key), 1)
                elif c in (C_AGATE, C_GGATE):
                    o = 0 if c == C_AGATE else ATT_W
                    before = t + (TILES if c == C_GGATE else 0)
                    if before > 0:
                        act.wait_ge(s["v_gate"], before)
                    nc.scalar.activation(th[:, :], b[:, :], ACT.Tanh, scale=hrstd)
                    nc.scalar.activation(xm[:, t, o:o + 512], b[:, :], ACT.Copy, scale=hrstd).then_inc(emptied(key), 1)
                else:
                    if c == C_GV and t == 0:
                        for odd in range(2):
                            wait_full(act, ("pairs", LEVELS - 1, odd))
                    dst = {C_AQ: row, C_AK: row, C_GQK: grow, C_AV: av, C_GV: gv}[c]
                    nc.scalar.activation(dst[:, t, :], b[:, :], ACT.Copy, scale=rstd).then_inc(emptied(key), 1)

            def idxT_(t):
                key = ("idxT", t)
                b = wait_full(act, key)
                nc.scalar.activation(idxT[:, :, P * t:P * (t + 1)], b[:, :].rearrange("p (k n) -> p k n", k=4),
                                     ACT.Copy).then_inc(emptied(key), 1)

            def score(t, h):
                key, n, i = ("score", t, h), (t + 1) * P, IDX_HEADS * (t - 1) + h
                b = wait_full(act, key)
                if i >= 2:
                    act.wait_ge(s["v_score"], (i - 2) // IDX_HEADS * 5 + (i - 2) % IDX_HEADS + 1)
                nc.scalar.activation(rel[:, i % 2, 0:n], b[:, 0:n], ACT.Relu).then_inc(emptied(key), 1)

            def logalpha():
                for t in range(TILES):
                    wait_moved(act, ("gz", t))
                nc.scalar.activation(lgt[:, :, :], lg[:, :, :], ACT.Abs).then_inc(s["a_la"], 1)
                act.wait_ge(s["a_la"], 1)
                nc.scalar.activation(lgt[:, :, :], lgt[:, :, :], ACT.Exp, scale=-1.0).then_inc(s["a_la"], 1)
                act.wait_ge(s["a_la"], 2)
                nc.scalar.activation(lgt[:, :, :], lgt[:, :, :], ACT.Ln, bias=1.0).then_inc(s["a_la"], 1)

            def cum(t):
                key = ("cum", t)
                b = wait_full(act, key)
                nc.scalar.activation(bT[:, :, P * t:P * (t + 1)], b[:, 0:256].rearrange("p (g n) -> p g n", g=2),
                                     ACT.Copy)
                nc.scalar.activation(lg[:, t, :], b[:, 256:512], ACT.Exp, scale=1 / 16).then_inc(emptied(key), 1)

            def rowT(c, t):
                key = ("rowT", c, t)
                b = wait_full(act, key)[:, :].rearrange("p (k n) -> p k n", k=4)
                if c == C_GQK:
                    nc.scalar.activation(gqkT[:, 0:2, P * t:P * (t + 1)], b[:, 0:2, :], ACT.Copy, scale=GLA_DK ** -0.5)
                    nc.scalar.activation(gqkT[:, 2:4, P * t:P * (t + 1)], b[:, 2:4, :], ACT.Copy)\
                        .then_inc(emptied(key), 1)
                else:
                    dst = aqT if c == C_AQ else akT
                    nc.scalar.activation(dst[:, :, P * t:P * (t + 1)], b, ACT.Copy).then_inc(emptied(key), 1)

            def exp_level(lev):
                half = P // 2 >> lev
                e = E[:, :, :].rearrange("p g (n i) -> p (g n) i", i=2 * half)
                act.wait_ge(s["v_D"], lev + 1)
                nc.scalar.activation(e[:, :, 0:half], e[:, :, 0:half], ACT.Exp, scale=-1 / 16).then_inc(s["a_E"], 1)
                nc.scalar.activation(e[:, :, half:], e[:, :, half:], ACT.Exp, scale=1 / 16).then_inc(s["a_E"], 1)

            def qinter():
                act.wait_ge(s["v_qk"], 3)
                wait_moved(act, ("cum", TILES - 1))
                nc.scalar.activation(E[:, :, :], bT[:, :, :], ACT.Exp, scale=1 / 16).then_inc(s["a_dec"], 1)
                act.wait_ge(s["a_dec"], 1)
                nc.scalar.activation(dec[:, :, :], E[:, :, P - 1::P], ACT.Copy).then_inc(s["a_dec"], 1)
                exp_level(0)

            def level(lev):
                if lev + 1 < LEVELS:
                    exp_level(lev + 1)

            def pairs(lev, odd):
                if lev > 0:
                    return
                key = ("pairs", lev, odd)
                b = wait_full(act, key)
                act.wait_ge(s["g_init"], 4)
                nc.scalar.activation(AT[0:64, odd::2, :, 64:128],
                                     b[0:64, :].rearrange("p (g t n) -> p g t n", g=GLA_HEADS // 2, t=TILES),
                                     ACT.Copy).then_inc(emptied(key), 1)

            def qk_(t, h):
                u, n = unit_no[(t, h)], (t + 1) * P
                wait_moved(act, ("qk", t, h))
                nc.scalar.activation(Pb[:, u % 2, 0:n], Pb[:, u % 2, 0:n], ACT.Exp, bias=nmax[:, u:u + 1], scale=-1.0,
                                     accum_out=psums[:, u:u + 1]).then_inc(s["a_p"], 1)

            def pT(t, h):
                u, n, key = unit_no[(t, h)], (t + 1) * P, ("pT", t, h)
                if not pT_on_act(u):
                    return
                b = wait_full(act, key)
                if u >= 2:
                    pv_done(act, u - 2)
                nc.scalar.activation(pTb[:, u % 2, 0:n], b[:, 0:n], ACT.Copy).then_inc(emptied(key), 1)

            def glaout(t):
                wait_moved(act, ("glaout", t, 0))
                wait_moved(act, ("glaout", t, 1))
                for h in range(GLA_HEADS):
                    if GLA_HEADS * t + h > 0:
                        act.wait_ge(s["a_gsq"], GLA_HEADS * t + h)
                    nc.scalar.activation(E[:, 0, 0:P], og[:, t % 2, P * h:P * (h + 1)], ACT.Square,
                                         accum_out=gss[:, 0, GLA_HEADS * t + h:GLA_HEADS * t + h + 1])\
                        .then_inc(s["a_gsq"], 1)

            def wprep(j):
                act.wait_ge(d_raw[j % 2], raw_value(2 * NC + j))
                if j == 0:
                    half_done(act, 2 * NC - 2)
                if 2 * j == KT // 2:
                    half_done(act, 2 * NC - 1)
                src = raw[:, j % 2, :, :].rearrange("p (k m) n -> p k (m n)", k=2)
                k = 2 * j
                nc.scalar.activation(hT_hi[:, k:k + 2, :], src[:, :, 0:512], ACT.Copy).then_inc(s["a_wo"], 1)
                nc.scalar.activation(w_hi[:, k // 4, k % 4:k % 4 + 2, :], src[:, :, 512:1024], ACT.Copy)\
                    .then_inc(s["a_wo"], 1)

            def mixT(t, g):
                b = wait_full(act, ("mixT", t, g))
                nc.scalar.activation(mT_hi[t][:, 4 * g:4 * g + 4, :], b[:, :].rearrange("p (k n) -> p k n", k=4),
                                     ACT.Copy).then_inc(s["a_mTh"], 1)

            def outp(t, n):
                b = wait_full(act, ("outp", t, n))
                if 2 * t + n > 0:
                    act.wait_ge(s["a_osq"], 2 * t + n)
                nc.scalar.activation(E[:, n, :], b[:, :], ACT.Square, accum_out=oss[:, n, t:t + 1])\
                    .then_inc(s["a_osq"], 1)

            parts = {"prep": prep, "xT": xT, "ssq": ssq_, "angles": angles, "evac": evac, "idxT": idxT_, "score": score,
                     "logalpha": logalpha, "cum": cum, "rowT": rowT, "qinter": qinter, "level": level, "pairs": pairs, "qk": qk_,
                     "pT": pT, "glaout": glaout, "wprep": wprep, "mixT": mixT, "outp": outp}
            for step in plan:
                if step[0] in parts:
                    parts[step[0]](*step[1:])

        @block.vector
        def _(dve):
            V = nc.vector

            def angles():
                a, turns, r, c = (ang[:, n, :, :] for n in range(4))
                magic = 1.5 * 2.0 ** 23
                steps = [
                    lambda: V.tensor_tensor(a, pos[:, :].unsqueeze(2).broadcast_to([P, TILES, HALF]),
                                            cst[:, FREQ:FREQ + HALF].unsqueeze(1).broadcast_to([P, TILES, HALF]),
                                            ALU.mult),
                    lambda: V.tensor_scalar(turns, a, 1 / (2 * PI), magic, ALU.mult, ALU.add),
                    lambda: V.tensor_scalar(turns, turns, -magic, None, ALU.add),
                    lambda: V.scalar_tensor_tensor(r, turns, -TWO_PI[0], a, ALU.mult, ALU.add),
                    lambda: V.scalar_tensor_tensor(r, turns, -TWO_PI[1], r, ALU.mult, ALU.add),
                    lambda: V.scalar_tensor_tensor(r, turns, -TWO_PI[2], r, ALU.mult, ALU.add),
                    lambda: V.tensor_scalar(r, r, PI_BELOW, -PI_BELOW, ALU.min, ALU.max),
                    lambda: V.scalar_tensor_tensor(c, r, -1.0, r, ALU.mult, ALU.min),
                    lambda: V.tensor_scalar(c, c, PI / 2, None, ALU.add),
                ]
                dve.wait_ge(d_pos, 16)
                dve.wait_ge(d_cst, 16)
                for n, step in enumerate(steps):
                    if n > 0:
                        dve.wait_ge(s["v_ang"], n)
                    step().then_inc(s["v_ang"], 1)

            def xT(t, g):
                key, j = ("xT", t, g), 2 * t + g
                b = wait_full(dve, key)
                if j == 0:
                    dve.wait_ge(d_prew, 16)
                if j >= 4:
                    dve.wait_ge(s["g_hTl"], j - 3)
                V.tensor_tensor(row[:, j % 4, :].rearrange("p (k n) -> p k n", k=4),
                                b[:, :].rearrange("p (k n) -> p k n", k=4),
                                prew[:, 4 * g:4 * g + 4].unsqueeze(2).broadcast_to([P, 4, P]),
                                ALU.mult).then_inc(emptied(key), 1)

            def prep(n):
                w = WIDTH[n // 2]
                dve.wait_ge(s["a_whi"], n + 1)
                V.tensor_tensor(w_lo[:, n % 2, :, 0:w], raw[:, n % 2, :, 0:w], w_hi[:, n % 2, :, 0:w].bitcast(F32),
                                ALU.subtract).then_inc(s["v_wlo"], 1)

            def evac(c, t):
                if c not in (C_AGATE, C_GGATE):
                    return
                o = 0 if c == C_AGATE else ATT_W
                wait_moved(dve, ("proj", c, t))
                g = xm[:, t, o:o + 512]
                V.scalar_tensor_tensor(g, th[:, :], 1.0, g, ALU.add, ALU.mult).then_inc(s["v_gate"], 1)

            def cand(t):
                at = sum((u + 1) * P for u in range(1, t))
                return work[:, at:at + (t + 1) * P]

            def bias_of(t):
                if t == 0:
                    return cst[:, CAUSAL:CAUSAL + P]
                at = sum((u + 1) * P for u in range(1, t))
                return bias[:, at:at + (t + 1) * P]

            def score(t, h):
                n, i = (t + 1) * P, IDX_HEADS * (t - 1) + h
                wait_moved(dve, ("score", t, h))
                dst, wt = cand(t), iw[:, t, h:h + 1]
                if h == 0:
                    V.tensor_scalar(dst, rel[:, i % 2, 0:n], wt, None, ALU.mult).then_inc(s["v_score"], 1)
                    return
                dve.wait_ge(s["v_score"], 5 * (t - 1) + h)
                V.scalar_tensor_tensor(dst, rel[:, i % 2, 0:n], wt, dst, ALU.mult, ALU.add).then_inc(s["v_score"], 1)
                if h == IDX_HEADS - 1:
                    dve.wait_ge(s["v_score"], 5 * (t - 1) + h + 1)
                    dst = dst[:, t * P:(t + 1) * P]
                    V.tensor_tensor(dst, dst, cst[:, CAUSAL:CAUSAL + P], ALU.add).then_inc(s["v_score"], 1)

            def topk(t, r):
                m = ROUNDS * (t - 1) + r
                if r == 0:
                    dve.wait_ge(s["v_score"], 5 * t)
                if m > 0:
                    dve.wait_ge(s["v_cand"], m)
                V.max(best[:, :], cand(t)).then_inc(s["v_best"], 1)
                dve.wait_ge(s["v_best"], m + 1)
                V.match_replace(cand(t), best[:, :], cand(t), TAKEN).then_inc(s["v_cand"], 1)
                if r == ROUNDS - 1:
                    dve.wait_ge(s["v_cand"], m + 1)
                    V.tensor_scalar(bias_of(t), cand(t), TAKEN, NEG, ALU.is_gt, ALU.mult).then_inc(s["v_bias"], 1)

            def gz(t):
                key = ("gz", t)
                b = wait_full(dve, key)
                if t == 0:
                    dve.wait_ge(d_small, 48)
                V.tensor_tensor(lg[:, t, :], b[:, 0:256], bgate[:, :], ALU.add).then_inc(emptied(key), 1)

            def logalpha():
                dve.wait_ge(s["a_la"], 3)
                V.scalar_tensor_tensor(lg[:, :, :], lg[:, :, :], 0.0, lgt[:, :, :], ALU.min, ALU.subtract)\
                    .then_inc(s["v_lg"], 1)

            def qkdiag():
                for t in range(TILES):
                    wait_moved(dve, ("proj", C_GQK, t))
                prod = E[:, :, :].rearrange("p g (t n) -> p (g t) n", n=256)
                V.tensor_tensor(prod, grow[:, :, 0:256], grow[:, :, 256:512], ALU.mult).then_inc(s["v_qk"], 1)
                dve.wait_ge(s["v_qk"], 1)
                V.tensor_reduce(qkd[:, 0, :], E[:, :, :].rearrange("p g (n d) -> p (g n) d", d=GLA_DK), AX.X,
                                ALU.add).then_inc(s["v_qk"], 1)
                dve.wait_ge(s["v_qk"], 2)
                V.tensor_scalar(qkd[:, 1, :], qkd[:, 0, :], GLA_DK ** -0.5, None, ALU.mult).then_inc(s["v_qk"], 1)

            def blocks(a, half):
                return a.rearrange("p g (n i) -> p (g n) i", i=2 * half)

            def diff(lev):
                half = P // 2 >> lev
                b, e = blocks(bT[:, :, :], half), blocks(E[:, :, :], half)
                n = 2 * SEQ // (2 * half)
                if lev == 0:
                    dve.wait_ge(s["v_qi"], 1)
                else:
                    dve.wait_ge(s["v_X"], 2 * lev)
                V.tensor_tensor(e, b, b[:, :, half - 1:half].broadcast_to([P, n, 2 * half]), ALU.subtract)\
                    .then_inc(s["v_D"], 1)

            def qinter():
                wait_moved(dve, ("rowT", C_GQK, TILES - 1))
                dve.wait_ge(s["a_dec"], 2)
                V.tensor_tensor(qi[:, :, :], gqkT[:, 0:2, :], E[:, :, :], ALU.mult).then_inc(s["v_qi"], 1)
                diff(0)

            def level(lev):
                half = P // 2 >> lev
                e, x = blocks(E[:, :, :], half), blocks(X[:, lev % 2, :, :], half)
                q, k = blocks(gqkT[:, 0:2, :], half), blocks(gqkT[:, 2:4, :], half)
                if lev >= 2:
                    for odd in range(2):
                        wait_full(dve, ("pairs", lev - 2, odd))
                dve.wait_ge(s["a_E"], 2 * (lev + 1))
                V.tensor_tensor(x[:, :, 0:half], k[:, :, 0:half], e[:, :, 0:half], ALU.mult).then_inc(s["v_X"], 1)
                V.tensor_tensor(x[:, :, half:], q[:, :, half:], e[:, :, half:], ALU.mult).then_inc(s["v_X"], 1)
                if lev + 1 < LEVELS:
                    diff(lev + 1)

            def pairs(lev, odd):
                if lev == 0:
                    return
                key = ("pairs", lev, odd)
                b = wait_full(dve, key)
                if lev == 1:
                    dve.wait_ge(s["g_init"], 4)
                for part in range(2):
                    at = slice(64 * part, 64 * part + 64)
                    last = V.copy_predicated(
                        AT[at, odd::2, :, at],
                        lvl[at, lev, at].unsqueeze(1).unsqueeze(1).broadcast_to([64, GLA_HEADS // 2, TILES, 64]),
                        b[at, :].rearrange("p (g t n) -> p g t n", g=GLA_HEADS // 2, t=TILES))
                last.then_inc(emptied(key), 1)

            def kv(t):
                if t == TILES - 1:
                    return
                key = ("kv", t)
                b = wait_full(dve, key)
                if t == 0:
                    V.tensor_copy(S[:, 0, :, :], b[:, 0:256].rearrange("p (g n) -> p g n", g=2))\
                        .then_inc(emptied(key), 1)
                    return
                wait_moved(dve, ("kv", t - 1))
                dve.wait_ge(s["a_dec"], 2)
                for g in range(2):
                    last = V.scalar_tensor_tensor(S[:, t, g, :], S[:, t - 1, g, :], dec[:, g, t:t + 1],
                                                  b[:, P * g:P * (g + 1)], ALU.mult, ALU.add)
                last.then_inc(emptied(key), 1)

            def glaout(t):
                dve.wait_ge(s["g_kt"], TILES - 1)
                if t >= 2:
                    dve.wait_ge(s["v_gm"], GLA_HEADS * (t - 1))
                for odd in range(2):
                    key = ("glaout", t, odd)
                    b = wait_full(dve, key)
                    for h in range(odd, GLA_HEADS, 2):
                        n = GLA_HEADS * t + h
                        last = V.scalar_tensor_tensor(og[:, t % 2, P * h:P * (h + 1)], gv[:, t, P * h:P * (h + 1)],
                                                      qkd[:, 1, n:n + 1], b[:, P * (h // 2):P * (h // 2 + 1)],
                                                      ALU.mult, ALU.add)
                    last.then_inc(emptied(key), 1)

            def glafin(t):
                dve.wait_ge(s["g_grs"], 2 * (t + 1))
                dve.wait_ge(s["g_gate"], t + 1)
                for h in range(GLA_HEADS):
                    n = GLA_HEADS * t + h
                    g = xm[:, t, ATT_W + P * h:ATT_W + P * (h + 1)]
                    V.scalar_tensor_tensor(g, og[:, t % 2, P * h:P * (h + 1)], gss[:, 2, n:n + 1], g, ALU.mult, ALU.mult)\
                        .then_inc(s["v_gm"], 1)

            def qk_(t, h):
                u, n, key = unit_no[(t, h)], (t + 1) * P, ("qk", t, h)
                b = wait_full(dve, key)
                if u >= 2:
                    wait_full(dve, ("pT", *UNITS[u - 2]))
                if h == 0 and t > 0:
                    dve.wait_ge(s["v_bias"], t)
                V.tensor_tensor_reduce(Pb[:, u % 2, 0:n], b[:, 0:n], bias_of(t), -ATT_HD ** -0.5, 3e38,
                                       ALU.add, ALU.min, nmax[:, u:u + 1]).then_inc(emptied(key), 1)

            def pT(t, h):
                u, n, key = unit_no[(t, h)], (t + 1) * P, ("pT", t, h)
                if pT_on_act(u):
                    return
                b = wait_full(dve, key)
                if u >= 2:
                    pv_done(dve, u - 2)
                V.tensor_copy(pTb[:, u % 2, 0:n], b[:, 0:n]).then_inc(emptied(key), 1)

            def attfin(t):
                key = ("att", t)
                dve.wait_ge(s["a_p"], ATT_HEADS * (t + 1))
                V.reciprocal(rinv[:, ATT_HEADS * t:ATT_HEADS * (t + 1)], psums[:, ATT_HEADS * t:ATT_HEADS * (t + 1)])\
                    .then_inc(s["v_rinv"], 1)
                b = wait_full(dve, key)
                dve.wait_ge(s["v_gate"], t + 1)
                V.tensor_tensor(xm[:, t, 0:ATT_W], b[:, :], xm[:, t, 0:ATT_W], ALU.mult).then_inc(emptied(key), 1)
                wait_moved(dve, key)
                dve.wait_ge(s["v_rinv"], t + 1)
                heads = xm[:, t, 0:ATT_W].rearrange("p (h n) -> p h n", h=ATT_HEADS)
                V.tensor_tensor(heads, heads, rinv[:, ATT_HEADS * t:ATT_HEADS * (t + 1)].unsqueeze(2)
                                .broadcast_to([P, ATT_HEADS, ATT_HD]), ALU.mult).then_inc(s["v_am"], 1)

            def wprep(j):
                src = raw[:, j % 2, :, :].rearrange("p (k m) n -> p k (m n)", k=2)
                k = 2 * j
                dve.wait_ge(s["a_wo"], 2 * j + 1)
                V.tensor_tensor(hT_lo[:, k:k + 2, :], src[:, :, 0:512], hT_hi[:, k:k + 2, :].bitcast(F32),
                                ALU.subtract).then_inc(s["v_wo"], 1)
                dve.wait_ge(s["a_wo"], 2 * j + 2)
                V.tensor_tensor(w_lo[:, k // 4, k % 4:k % 4 + 2, :], src[:, :, 512:1024],
                                w_hi[:, k // 4, k % 4:k % 4 + 2, :].bitcast(F32), ALU.subtract)\
                    .then_inc(s["v_wo"], 1)

            def mixT(t, g):
                key = ("mixT", t, g)
                dve.wait_ge(s["a_mTh"], 2 * t + g + 1)
                b = bank[jobs[key][0]]
                V.tensor_tensor(mT_lo[t][:, 4 * g:4 * g + 4, :], b[:, :].rearrange("p (k n) -> p k n", k=4),
                                mT_hi[t][:, 4 * g:4 * g + 4, :].bitcast(F32), ALU.subtract)\
                    .then_inc(emptied(key), 1)

            def weighted(t, n):
                key = ("outp", t, n)
                b = wait_full(dve, key)
                dve.wait_ge(s["a_osq"], 2 * t + n + 1)
                cols = slice(512 * n, 512 * (n + 1))
                V.tensor_tensor(yout[:, t % 2, cols], b[:, :], postw[:, cols], ALU.mult).then_inc(emptied(key), 1)

            def outp(t, n):
                if n > 0:
                    return
                if t == 0:
                    dve.wait_ge(d_post, 16)
                if t >= 2:
                    dve.wait_ge(d_out[t % 2], 32 * (t // 2))
                weighted(t, 0)

            def fin(t):
                c = slice(t, t + 1)
                dve.wait_ge(s["a_osq"], 2 * (t + 1))
                dve.wait_ge(s["g_ors"], 2 * t + 1)
                V.scalar_tensor_tensor(oss[:, 3, c], oss[:, 1, c], 1 / D_MODEL, oss[:, 2, c], ALU.mult, ALU.add)\
                    .then_inc(s["v_mean"], 1)
                weighted(t, 1)
                dve.wait_ge(s["g_ors"], 2 * t + 2)
                dve.wait_ge(d_xre[t % 2], 16 * (t // 2 + 1))
                for n in range(2):
                    wait_moved(dve, ("outp", t, n))
                    y = yout[:, t % 2, 512 * n:512 * (n + 1)]
                    V.scalar_tensor_tensor(y, y, oss[:, 4, c], xre[:, t % 2, 512 * n:512 * (n + 1)],
                                           ALU.mult, ALU.add).then_inc(s["v_y"], 1)

            parts = {"prep": prep, "xT": xT, "angles": angles, "evac": evac, "score": score, "topk": topk, "gz": gz,
                     "logalpha": logalpha, "qkdiag": qkdiag, "qinter": qinter, "level": level, "pairs": pairs,
                     "kv": kv, "glaout": glaout, "glafin": glafin, "qk": qk_, "pT": pT, "attfin": attfin,
                     "wprep": wprep, "mixT": mixT, "outp": outp, "fin": fin}
            for step in plan:
                if step[0] in parts:
                    parts[step[0]](*step[1:])

        @block.gpsimd
        def _(pool):
            G = nc.gpsimd
            G.memset(pwr[:, :], -0.5).then_inc(s["g_init"], 1)
            G.memset(idxrow[:, :, IW0 + IDX_HEADS:], 0.0).then_inc(s["g_init"], 1)
            roped = [0]

            def masks():
                pool.wait_ge(d_mask, 16)
                G.tensor_copy(lvl[:, :, :], lvl_in[:, :, :]).then_inc(s["g_init"], 1)
                pool.wait_ge(s["g_init"], 3)
                G.memset(AT[:, :, :, :], 0.0).then_inc(s["g_init"], 1)

            def xT(t, g):
                j = 2 * t + g
                pool.wait_ge(s["a_hTh"], j + 1)
                at = (slice(None), slice(4 * g, 4 * g + 4), slice(P * t, P * (t + 1)))
                G.tensor_tensor(hT_lo[at], row[:, j % 4, :].rearrange("p (k n) -> p k n", k=4),
                                hT_hi[at].bitcast(F32), ALU.subtract).then_inc(s["g_hTl"], 1)

            def ssq_(t):
                if t < TILES - 1:
                    return
                pool.wait_ge(s["g_init"], 2)
                pool.wait_ge(s["a_ssq"], TILES)
                G.tensor_scalar(ssq[:, 1, :], ssq[:, 0, :], 1 / D_MODEL, EPS, ALU.mult, ALU.add)\
                    .then_inc(s["g_rstd"], 1)
                pool.wait_ge(s["g_rstd"], 1)
                G.tensor_tensor(ssq[:, 2, :], ssq[:, 1, :], pwr[:, :].broadcast_to([P, TILES]), ALU.pow)\
                    .then_inc(s["g_rstd"], 1)
                pool.wait_ge(s["g_rstd"], 2)
                G.tensor_scalar(ssq[:, 3, :], ssq[:, 2, :], 0.5, None, ALU.mult).then_inc(s["g_rstd"], 1)

            def rope(a, t):
                heads = a.shape[1]
                x4 = a[:, :, 0:2 * HALF]
                by_cos, by_sin = (ropet[:, n, 0:heads, :] for n in range(2))
                over = [P, heads, HALF]
                if roped[0] > 0:
                    pool.wait_ge(s["g_rope"], roped[0])
                else:
                    pool.wait_ge(s["a_ang"], 4)
                roped[0] += 1
                G.tensor_tensor(by_cos, x4, cosd[:, t, :, :].rearrange("p a b -> p (a b)").unsqueeze(1)
                                .broadcast_to([P, heads, 2 * HALF]), ALU.mult).then_inc(s["g_ropet"], 1)
                for n in range(2):
                    G.tensor_tensor(by_sin[:, :, HALF * n:HALF * (n + 1)], x4[:, :, HALF * (1 - n):HALF * (2 - n)],
                                    sind[:, t, n, :].unsqueeze(1).broadcast_to(over), ALU.mult)\
                        .then_inc(s["g_ropet"], 1)
                pool.wait_ge(s["g_ropet"], 3 * roped[0])
                return G.tensor_tensor(x4, by_cos, by_sin, ALU.add)

            def evac(c, t):
                if c == C_IDX:
                    wait_moved(pool, ("proj", c, t))
                    rope(idxrow[:, t, 0:320].rearrange("p (h n) -> p h n", h=5), t).then_inc(s["g_iw"], 1)
                    G.tensor_scalar(iw[:, t, :], idxrow[:, t, IW0:IW0 + IDX_HEADS], (IDX_HEADS * IDX_HD) ** -0.5, None,
                                    ALU.mult).then_inc(s["g_iw"], 1)
                    pool.wait_ge(s["g_iw"], 2 * (t + 1))
                    G.tensor_copy(idxrow[:, t, 320:384], idxrow[:, t, 256:320]).then_inc(s["g_rope"], 1)
                elif c in (C_AQ, C_AK):
                    wait_moved(pool, ("proj", c, t))
                    rope(row[:, t, :].rearrange("p (h n) -> p h n", h=ATT_HEADS), t).then_inc(s["g_rope"], 1)
                elif c == C_GGATE:
                    pool.wait_ge(s["v_gate"], TILES + t + 1)
                    if t == 0:
                        pool.wait_ge(d_small, 48)
                    g = xm[:, t, ATT_W:].rearrange("p (h n) -> p h n", h=GLA_HEADS)
                    G.tensor_tensor(g, g, glaw[:, :].unsqueeze(1).broadcast_to([P, GLA_HEADS, GLA_DV]), ALU.mult)\
                        .then_inc(s["g_gate"], 1)

            def level(lev):
                if lev > 0:
                    return
                pool.wait_ge(s["v_qk"], 3)
                for t in range(TILES - 1):
                    wait_moved(pool, ("rowT", C_GQK, t))
                    wait_moved(pool, ("cum", t))
                    k = grow[:, t, 256:512]
                    G.tensor_tensor(k, k, lg[:, t, :], ALU.mult).then_inc(s["g_kt"], 1)

            def glaout(t):
                n = GLA_HEADS * t
                pool.wait_ge(s["a_gsq"], n + GLA_HEADS)
                G.tensor_scalar(gss[:, 1, n:n + 4], gss[:, 0, n:n + 4], 1 / GLA_DV, EPS, ALU.mult, ALU.add)\
                    .then_inc(s["g_grs"], 1)
                pool.wait_ge(s["g_grs"], 2 * t + 1)
                G.tensor_tensor(gss[:, 2, n:n + 4], gss[:, 1, n:n + 4], pwr[:, :].broadcast_to([P, 4]), ALU.pow)\
                    .then_inc(s["g_grs"], 1)

            def outp(t, n):
                if n > 0:
                    return
                pool.wait_ge(s["a_osq"], 2 * t + 1)
                c = slice(t, t + 1)
                G.tensor_scalar(oss[:, 2, c], oss[:, 0, c], 1 / D_MODEL, EPS, ALU.mult, ALU.add)\
                    .then_inc(s["g_ors"], 1)

            def fin(t):
                c = slice(t, t + 1)
                pool.wait_ge(s["v_mean"], t + 1)
                G.tensor_tensor(oss[:, 4, c], oss[:, 3, c], pwr[:, :], ALU.pow).then_inc(s["g_ors"], 1)

            parts = {"masks": masks, "xT": xT, "ssq": ssq_, "evac": evac, "level": level, "glaout": glaout,
                     "outp": outp, "fin": fin}
            for step in plan:
                if step[0] in parts:
                    parts[step[0]](*step[1:])


def kernel(**inputs):
    import numpy as np
    import concourse.bacc as bacc
    from concourse.bass_utils import run_bass_kernel_spmd as run

    nc = bacc.Bacc("TRN2", target_bir_lowering=False, num_devices=1)
    i = np.arange(P)
    consts = np.zeros((P, NCONST), np.float32)
    consts[:, IDENT:IDENT + P] = np.eye(P)
    consts[:, CUM:CUM + P] = i[:, None] <= i[None, :]
    consts[:, REV:REV + P] = i[:, None] > i[None, :]
    consts[:, CAUSAL:CAUSAL + P] = np.where(i[None, :] <= i[:, None], 0.0, NEG)
    freq = np.float32(500000.0) ** (-np.arange(0, 2 * HALF, 2, dtype=np.float32) / np.float32(2 * HALF))
    consts[:, FREQ:FREQ + HALF] = freq
    far = i[:, None] ^ i[None, :]
    masks = np.stack([(far >> (LEVELS - 1 - lev) == 1) & (i[None, :] > i[:, None]) for lev in range(LEVELS)], 1)
    arrays, aps = {}, []
    for name in ("x", "positions", "w_in", "w_gla_gate_up", "b_gla_gate", "gla_norm_w", "w_out", "pre_norm_w",
                 "post_norm_w"):
        arrays["in_" + name] = np.ascontiguousarray(inputs[name])
    arrays["in_positions"] = np.ascontiguousarray(arrays["in_positions"].reshape(TILES, P).T)
    arrays["in_consts"] = consts
    arrays["in_masks"] = masks.astype(np.int32)
    for name, a in arrays.items():
        aps.append(nc.dram_tensor(name, a.shape, mybir.dt.from_np(a.dtype), kind="ExternalInput").ap())
    out = nc.dram_tensor("out", (1, SEQ, D_MODEL), F32, kind="ExternalOutput").ap()
    layer_kernel(nc, *aps, out)
    return run(nc, [arrays], core_ids=[0]).results[0]["out"]
```

```python
from contextlib import ExitStack

import concourse.bass as bass
from concourse import mybir

P = 128
SEQ, D_MODEL = 512, 1024
TILES = SEQ // P
KT = D_MODEL // P
ATT_HEADS, ATT_HD = 8, 64
IDX_HEADS, IDX_HD = 4, 64
GLA_HEADS, GLA_DK, GLA_DV, GATE_RANK = 4, 64, 128, 16
ATT_W, GLA_W = ATT_HEADS * ATT_HD, GLA_HEADS * GLA_DV
HALF = ATT_HD // 4 // 2
KSEL = SEQ // 4
ROUNDS = KSEL // 8
EPS = 1e-6
NEG = -1e30
TAKEN = -3e38
LEVELS = 7
PI = 3.141592653589793
PI_BELOW = 3.1415925
TWO_PI = (6.28125, 0.0019350051879882812, 3.0199159819e-07)

F32 = mybir.dt.float32
F32R = mybir.dt.float32r
I32 = mybir.dt.int32
U8 = mybir.dt.uint8
ALU = mybir.AluOpType
ACT = mybir.ActivationFunctionType
AX = mybir.AxisListType

CHUNKS = [
    [(1536, 324), (3396, 16)],
    [(2372, 512)],
    [(0, 512)],
    [(512, 512)],
    [(1024, 512)],
    [(1860, 512)],
    [(2884, 512)],
    [(3412, 512)],
]
C_IDX, C_GQK, C_AQ, C_AK, C_AV, C_AGATE, C_GV, C_GGATE = range(8)
NC = len(CHUNKS)
WIDTH = [sum(w for _, w in c) for c in CHUNKS]
WOUT_PIECES = 4
LR0, IW0 = 384, 400
IDENT, CUM, REV, CAUSAL, FREQ, NCONST = 0, 128, 256, 384, 512, 520

GENERAL = [4, 5, 6, 7]
OUT_BANKS = [2, 3]
O_BANK = 7


def pT_on_act(u):
    return u % 2 == 0


def low_on_pool(n):
    return n > 1 and n % 2 == 1 or n > 8


def units(tiles):
    return [(t, h) for t in tiles for h in range(ATT_HEADS)]


def schedule():
    groups = [(c, half, t) for c in range(NC) for half in range(2) for t in range(TILES)]
    fill = {g: [] for g in groups}

    def at(c, half, t, *steps):
        fill[(c, half, t)].extend(steps)

    for t in range(TILES):
        at(C_IDX + 1, 0, t, ("idxT", t))
        at(*groups[groups.index((C_IDX + 1, 0, 1)) + t], ("gz", t))
        at(C_GQK + 1, 0, t, ("rowT", C_GQK, t), ("cum", t))
        at(C_AQ + 1, 0, t, ("rowT", C_AQ, t))
        at(C_AK + 1, 0, t, ("rowT", C_AK, t))
        at(C_GV + 1, 0, t, ("kv", t))
    first = groups.index((C_IDX + 1, 0, 2))
    for n in range((TILES - 1) * IDX_HEADS):
        at(*groups[first + n // 2], ("score", n // IDX_HEADS + 1, n % IDX_HEADS))
    at(C_IDX + 1, 0, 3, ("masks",))
    at(C_IDX + 1, 1, 0, ("logalpha",))
    at(C_GQK + 1, 0, 0, ("qkdiag",))
    at(C_GQK + 1, 1, 0, ("qinter",))
    at(C_GQK + 1, 1, 1, ("level", 0))
    at(C_GQK + 1, 1, 2, ("decay", 1))
    first = groups.index((C_AV + 1, 0, 0))
    for n, u in enumerate(units(range(TILES - 1))):
        at(*groups[first + n], ("unit", *u))
    at(C_AK + 1, 1, 0, ("qparts", 0, 0))
    first, last = groups.index((C_GQK + 1, 1, 3)), groups.index((C_GV, 0, 0))
    for n in range(2 * LEVELS):
        lev, odd = divmod(n, 2)
        g = first + n * (last - first) // (2 * LEVELS - 1)
        if odd == 0 and lev > 0:
            at(*groups[g - 2], ("level", lev))
            at(*groups[g - 1], ("decay", lev + 1))
        at(*groups[g], ("pairs", lev, odd))
    at(NC - 1, 1, 1, ("glaout", 0), ("glasum", 0))
    at(NC - 1, 1, 2, ("glafin", 0))
    at(NC - 1, 1, 3, ("glaout", 1), ("mixT", 0, 0), ("mixT", 0, 1), ("glasum", 1))
    for n in range(4):
        at(NC - 1, 1, n * 3 // 4, ("wprep", n // 2, n % 2))

    first = groups.index((C_IDX + 1, 1, 1))
    rounds = [("topk", t, r) for t in range(1, TILES) for r in range(ROUNDS)]
    for n, step in enumerate(rounds):
        at(*groups[first + n * 7 // 8], step)

    plan = [("xT", 0, 0), ("xT", 0, 1), ("prep", 0), ("ssq", 0), ("ssq", 1), ("xT", 1, 0), ("xT", 1, 1)]
    for c, half, t in groups:
        plan.append(("proj", c, half, t))
        n = 2 * c + half
        if n == 0:
            plan += [[("ssq", 2), ("xT", 2, 0), ("xT", 2, 1)], [("xT", 3, 0), ("xT", 3, 1), ("prep", 1), ("ssq", 3)],
                     [("angles",)], []][t]
        elif t == 0 and n < 2 * NC - 1:
            plan.append(("prep", n + 1))
        if half == 1:
            plan.append(("evac", c, t))
        plan += fill[(c, half, t)]
    between = [[("outp", 0, 0, 0), ("wprep", 2, 0), ("wprep", 2, 1), ("glafin", 1)],
               [("outp", 0, 1, 0), ("wprep", 3, 0), ("glaout", 2)],
               [("mixT", 1, 0), ("mixT", 1, 1), ("wprep", 3, 1), ("glasum", 2)],
               [("glaout", 3), ("glafin", 2)],
               [("glasum", 3), ("outp", 0, 0, 1), ("glafin", 3)],
               [("outp", 0, 1, 1), ("fin", 0), ("mixT", 2, 0), ("mixT", 2, 1)],
               [("outp", 1, 0, 0), ("outp", 1, 0, 1)], []]
    for u, steps in zip(units([TILES - 1]), between):
        plan.append(("unit", *u))
        plan += steps
    outputs = [("outp", t, n, half) for t in range(1, TILES) for n in range(2) for half in range(2)]
    plan += [outputs[2], ("behind",), outputs[3], ("fin", 1), ("behind",), *outputs[4:6], ("mixT", 3, 0),
             ("mixT", 3, 1), *outputs[6:8], ("fin", 2), *outputs[8:], ("fin", 3)]

    out, all_units, n = [], units(range(TILES)), 0
    for step in plan:
        if step[0] not in ("unit", "behind"):
            out.append(step)
            continue
        if step[0] == "unit":
            out.append(("qk", *step[1:]))
        if 0 < n <= len(all_units):
            out.append(("pT", *all_units[n - 1]))
        if n > 1:
            out.append(("pv", *all_units[n - 2]))
            if all_units[n - 2][1] == ATT_HEADS - 1:
                out.append(("attfin", all_units[n - 2][0]))
        if n + 2 < len(all_units) and all_units[n + 2][1] % 2 == 0:
            out.append(("qparts", *all_units[n + 2]))
        n += 1
    return out


def psum_jobs(plan):
    jobs, used, ring = {}, [0] * 8, list(GENERAL)

    def take(key, bank):
        jobs[key] = (bank, used[bank])
        used[bank] += 1

    def take_next(key):
        ring.append(ring.pop(0))
        take(key, ring[-1])

    for s in plan:
        if s[0] == "proj" and s[2] == 0:
            take(("proj", s[1], s[3]), s[3])
        elif s[0] in ("xT", "idxT", "score", "gz", "rowT", "cum", "pairs", "qk", "pT", "mixT"):
            take_next(s)
        elif s[0] == "kv" and s[1] < TILES - 1:
            take_next(s)
        elif s[0] == "glaout":
            for odd in range(2):
                take_next((*s, odd))
        elif s[0] == "pv" and s[2] == 0:
            if O_BANK in ring:
                ring.remove(O_BANK)
            take(("att", s[1]), O_BANK)
        elif s[0] == "outp" and s[3] == 0:
            take(s[:3], OUT_BANKS[s[2]])
        elif s[0] == "evac" and s[1] == NC - 1 and s[2] not in OUT_BANKS:
            ring.append(s[2])
    return jobs


def layer_kernel(nc, x, positions, w_in, w_up, b_gate, gla_norm_w, w_out, pre_norm_w, post_norm_w,
                 consts, level_masks, out):
    plan = schedule()
    jobs = psum_jobs(plan)
    UNITS = [s[1:] for s in plan if s[0] == "qk"]
    unit_no = {u: n for n, u in enumerate(UNITS)}
    PAIRS = [s[1:] for s in plan if s[0] == "pairs"]
    x_v = x.rearrange("b (t p) d -> (b t) p d", p=P)
    out_v = out.rearrange("b (t p) d -> (b t) p d", p=P)
    w_in_v = w_in.rearrange("(p k) n -> p k n", k=KT)
    w_out_v = w_out.rearrange("(p k) n -> p k n", k=KT)

    with ExitStack() as ctx:
        place = [(nc.sbuf_base + 63) // 32 * 32]

        def put(name, shape, dt=F32, offset=None):
            size = {F32: 4, F32R: 4, I32: 4, U8: 1}[dt]
            for n in shape[1:]:
                size *= n
            at = place[0] if offset is None else offset
            if offset is None:
                place[0] += (size + 31) // 32 * 32
            return nc.alloc_sbuf_tensor_at(name, shape, dt, offset=at), at

        def sb(name, shape, dt=F32, offset=None):
            return put(name, shape, dt, offset)[0]

        def sem(name):
            return ctx.enter_context(nc.semaphore(name))

        cst, cst_at = put("cst", [P, NCONST])
        lvl = sb("lvl", [P, LEVELS, P], U8)
        prew = sb("prew", [P, KT])
        glaw = sb("glaw", [P, GLA_DV])
        bgate, bgate_at = put("bgate", [P, GLA_HEADS * GLA_DK])
        qT_parts = [sb(f"qT_parts{n}", [P, 2, P], F32R, offset=at) for n, at in enumerate((cst_at + 4 * CUM, bgate_at))]
        wup = sb("wup", [GATE_RANK, GLA_HEADS * GLA_DK])
        pos = sb("pos", [P, TILES], I32)
        ang = sb("ang", [P, 4, TILES, HALF])
        cosd = sb("cosd", [P, TILES, 2, HALF])
        sind = sb("sind", [P, TILES, 2, HALF])
        ropet = sb("ropet", [P, 2, ATT_HEADS, 2 * HALF])
        ssq = sb("ssq", [P, 4, TILES])
        iw = sb("iw", [P, TILES, IDX_HEADS])
        best = sb("best", [P, 8])
        nmax = sb("nmax", [P, TILES * ATT_HEADS])
        psums = sb("psums", [P, TILES * ATT_HEADS])
        rinv = sb("rinv", [P, TILES * ATT_HEADS])
        qkd = sb("qkd", [P, 2, TILES * GLA_HEADS])
        dec = sb("dec", [P, 2, TILES])
        gss = sb("gss", [P, 3, TILES * GLA_HEADS])
        oss = sb("oss", [P, 5, TILES])
        pwr = sb("pwr", [P, 1])
        xm = sb("xm", [P, TILES, D_MODEL])
        hT_hi = sb("hT_hi", [P, KT, SEQ], F32R)
        hT_lo = sb("hT_lo", [P, KT, SEQ], F32R)
        w_hi = sb("w_hi", [P, 2, KT // 2, 512], F32R)
        w_lo = sb("w_lo", [P, 2, KT // 2, 512], F32R)
        raw, raw_at = put("raw", [P, 2, KT // 2, 512])
        aqT, aq_at = put("aqT", [P, 4, SEQ])
        kT_hi, ak_at = put("kT_hi", [P, ATT_HEADS // 2, SEQ], F32R)
        kT_lo = sb("kT_lo", [P, ATT_HEADS // 2, SEQ], F32R)
        iqT = sb("iqT", [P, IDX_HEADS, SEQ], F32R, offset=aq_at)
        ikT_hi = sb("ikT_hi", [P, SEQ], F32R, offset=ak_at)
        ikT_lo = sb("ikT_lo", [P, SEQ], F32R, offset=ak_at + 4 * SEQ)
        lrT = sb("lrT", [GATE_RANK, SEQ], offset=ak_at + 8 * SEQ)
        av, av_at = put("av", [P, TILES, ATT_W])
        row = sb("row", [P, TILES, 512], offset=av_at)
        idxrow, idx_at = put("idxrow", [P, TILES, 512])
        bT, bT_at = put("bT", [P, 2, SEQ])
        qi = sb("qi", [P, 2, SEQ])
        gqkT = sb("gqkT", [P, 4, SEQ], offset=idx_at)
        yout = sb("yout", [P, 2, D_MODEL], offset=idx_at)
        xre = sb("xre", [P, 2, D_MODEL], offset=bT_at)
        work, work_at = put("work", [P, 1152])
        postw = sb("postw", [P, D_MODEL], offset=work_at)
        bias = sb("bias", [P, 1280])
        grow, grow_at = put("grow", [P, TILES, 512])
        gv, gv_at = put("gv", [P, TILES, GLA_W])
        X = sb("X", [P, 2, 2, SEQ], offset=gv_at)
        lg, lg_at = put("lg", [P, TILES, 256])
        og = sb("og", [P, 2, 512], offset=lg_at)
        Pb, p_at = put("Pb", [P, 2, 512])
        lgt = sb("lgt", [P, TILES, 256], offset=p_at)
        pTb, pt_at = put("pTb", [P, 2, 512])
        rel = sb("rel", [P, 2, 512], offset=pt_at)
        E = sb("E", [P, 2, SEQ])
        AT, at_at = put("AT", [P, GLA_HEADS, TILES, P])
        lvl_in = sb("lvl_in", [P, LEVELS, P], I32, offset=at_at)
        mT_hi, mT_lo = ([sb(f"mT_{part}{t}", [P, KT, P], F32R, offset=at + 4 * P * KT * n)
                         for t, (at, n) in enumerate(places)] for part, places in (
            ("hi", [(idx_at, 1), (raw_at, 0), (at_at, 0), (gv_at, 0)]),
            ("lo", [(grow_at, 0), (grow_at, 1), (at_at, 1), (gv_at, 1)])))
        S = sb("S", [P, TILES - 1, 2, GLA_DV])
        th = sb("th", [P, 512])
        assert place[0] <= nc.sbuf_usable_end, place[0] - nc.sbuf_usable_end

        bank = [ctx.enter_context(nc.psum_tensor(f"bank{n}", [P, 512], F32)) for n in range(8)]
        full = [sem(f"bank{n}_full") for n in range(8)]
        moved = [sem(f"bank{n}_moved") for n in range(8)]

        d_ident, d_cst, d_prew, d_small, d_mask, d_pos, d_post = (sem(n) for n in (
            "d_ident", "d_cst", "d_prew", "d_small", "d_mask", "d_pos", "d_post"))
        d_x = [sem(f"d_x{t}") for t in range(TILES)]
        d_raw = [sem(f"d_raw{n}") for n in range(2)]
        d_xre = [sem(f"d_xre{n}") for n in range(2)]
        d_out = [sem(f"d_out{n}") for n in range(2)]
        names = ("a_ssq a_iT a_kh a_qh a_hTh a_whi a_ang a_la a_dec a_E a_p a_gsq a_mTh a_osq a_wo "
                 "v_hTl v_wlo v_ang v_score v_cand v_best v_bias v_lg v_gate v_qk v_qi v_D v_X "
                 "v_gm v_rinv v_am v_mean v_y v_wo "
                 "g_init g_ql g_wlo g_wo g_hTl g_rstd g_ropet g_rope g_iw g_kt g_gate g_grs g_ors t_half t_pv").split()
        s = {n: sem(n) for n in names}

        def raw_value(n):
            pieces = [len(CHUNKS[m // 2]) if m < 2 * NC else 1 for m in range(n % 2, n + 1, 2)]
            return 16 * sum(pieces)

        def wait_full(eng, key):
            b, n = jobs[key]
            eng.wait_ge(full[b], n + 1)
            return bank[b]

        def is_free(eng, key):
            b, n = jobs[key]
            if n > 0:
                eng.wait_ge(moved[b], n)
            return bank[b]

        def wait_moved(eng, key):
            b, n = jobs[key]
            eng.wait_ge(moved[b], n + 1)

        def half_done(eng, n):
            c, half = divmod(n, 2)
            if half == 0:
                eng.wait_ge(s["t_half"], c + 1)
            else:
                wait_full(eng, ("proj", c, TILES - 1))

        def low_done(eng, n):
            if low_on_pool(n):
                eng.wait_ge(s["g_wlo"], sum(low_on_pool(m) for m in range(n + 1)))
            else:
                eng.wait_ge(s["v_wlo"], sum(not low_on_pool(m) for m in range(n + 1)))

        def pv_done(eng, n):
            t, h = UNITS[n]
            if h == ATT_HEADS - 1:
                wait_full(eng, ("att", t))
            else:
                eng.wait_ge(s["t_pv"], n - t)

        def filled(key):
            return full[jobs[key][0]]

        def emptied(key):
            return moved[jobs[key][0]]

        def ident():
            return cst[:, IDENT:IDENT + P]

        block = ctx.enter_context(nc.Block())

        @block.sync
        def _(sp):
            def load_weights(n):
                if n >= 2:
                    if n - 2 < 2 * NC:
                        sp.wait_ge(s["a_whi"], n - 1)
                        low_done(sp, n - 2)
                    else:
                        j = n - 2 * NC - 2
                        sp.wait_ge(s["a_wo"], 2 * (j + 1))
                        sp.wait_ge(s["v_wo"], j + 1)
                        sp.wait_ge(s["g_wo"], j + 1)
                if n < 2 * NC:
                    c, half = divmod(n, 2)
                    col = 0
                    for first, width in CHUNKS[c]:
                        sp.dma_start(raw[:, n % 2, :, col:col + width],
                                     w_in_v[:, half * KT // 2:(half + 1) * KT // 2, first:first + width]
                                     ).then_inc(d_raw[n % 2], 16)
                        col += width
                else:
                    j = n - 2 * NC
                    sp.dma_start(raw[:, n % 2, :, :].rearrange("p k n -> p (k n)"),
                                 w_out_v[:, 2 * j:2 * j + 2, :].rearrange("p k n -> p (k n)")
                                 ).then_inc(d_raw[n % 2], 16)

            sp.dma_start(xm[:, 0, :], x_v[0]).then_inc(d_x[0], 16)
            sp.dma_start(cst[:, 0:P], consts[:, 0:P]).then_inc(d_ident, 16)
            load_weights(0)
            for t in range(1, TILES):
                if t == TILES - 1:
                    load_weights(1)
                sp.dma_start(xm[:, t, :], x_v[t]).then_inc(d_x[t], 16)
            sp.dma_start(cst[:, P:], consts[:, P:]).then_inc(d_cst, 16)
            sp.dma_start(lvl_in[:, :, :], level_masks).then_inc(d_mask, 16)
            for n in range(2, 2 * NC + WOUT_PIECES):
                load_weights(n)
            sp.wait_ge(s["v_bias"], TILES - 1)
            sp.dma_start(postw[:, :], post_norm_w.partition_broadcast(P)).then_inc(d_post, 16)
            wait_moved(sp, ("glaout", TILES - 1, 1))
            for t in range(2):
                sp.dma_start(xre[:, t % 2, :], x_v[t]).then_inc(d_xre[t % 2], 16)
            for t in range(TILES):
                for n in range(2):
                    cols = slice(512 * n, 512 * (n + 1))
                    sp.wait_ge(s["v_y"], 2 * t + n + 1)
                    sp.dma_start(out_v[t][:, cols], yout[:, t % 2, cols]).then_inc(d_out[t % 2], 16)
                if t + 2 < TILES:
                    sp.dma_start(xre[:, t % 2, :], x_v[t + 2]).then_inc(d_xre[t % 2], 16)
            for n in range(2):
                sp.wait_ge(d_out[n], 16 * TILES)

        @block.tensor
        def _(pe):
            def xT(t, g):
                if g == 0:
                    pe.wait_ge(d_x[t], 16)
                    if t == 0:
                        pe.wait_ge(d_ident, 16)
                b = is_free(pe, ("xT", t, g))
                for j in range(4):
                    k = 4 * g + j
                    last = nc.tensor.transpose(b[:, P * j:P * (j + 1)], xm[:, t, k::KT], ident())
                last.then_inc(filled(("xT", t, g)), 1)

            def proj(c, half, t):
                n, w = 2 * c + half, WIDTH[c]
                b = bank[t]
                if t == 0:
                    pe.wait_ge(s["a_whi"], n + 1)
                    low_done(pe, n)
                if n == 0:
                    pe.wait_ge(s["g_hTl"], t + 1)
                    pe.wait_ge(s["v_hTl"], t + 1)
                if half == 0:
                    is_free(pe, ("proj", c, t))
                for j in range(KT // 2):
                    k = half * (KT // 2) + j
                    h_hi, h_lo = (a[:, k, P * t:P * (t + 1)] for a in (hT_hi, hT_lo))
                    v_hi, v_lo = (a[:, n % 2, j, 0:w] for a in (w_hi, w_lo))
                    nc.tensor.matmul(b[:, 0:w], h_hi, v_hi, start=(k == 0), stop=False)
                    nc.tensor.matmul(b[:, 0:w], h_hi, v_lo, start=False, stop=False)
                    last = nc.tensor.matmul(b[:, 0:w], h_lo, v_hi, start=False, stop=(k == KT - 1))
                if half == 1:
                    last.then_inc(full[t], 1)
                if half == 0 and t == TILES - 1:
                    last.then_inc(s["t_half"], 1)

            def idxT_(t):
                pe.wait_ge(s["g_rope"], t + 1)
                b = is_free(pe, ("idxT", t))
                for j in range(3):
                    nc.tensor.transpose(b[:, P * j:P * (j + 1)], idxrow[:, t, P * j:P * (j + 1)], ident())
                nc.tensor.transpose(b[0:GATE_RANK, 3 * P:4 * P], idxrow[:, t, LR0:LR0 + GATE_RANK], ident())\
                    .then_inc(filled(("idxT", t)), 1)

            def score(t, h):
                n, half = (t + 1) * P, slice(64 * (h % 2), 64 * (h % 2) + 64)
                if h == 0:
                    wait_moved(pe, ("idxT", t))
                b = is_free(pe, ("score", t, h))
                tile = slice(P * t, P * (t + 1))
                nc.tensor.matmul(b[:, 0:n], iqT[:, h, tile], ikT_hi[:, 0:n], start=True, stop=False)
                nc.tensor.matmul(b[:, 0:n], iqT[half, h, tile], ikT_lo[half, 0:n],
                                 start=False, stop=True).then_inc(filled(("score", t, h)), 1)

            def gz(t):
                wait_moved(pe, ("idxT", t))
                if t == 0:
                    pe.wait_ge(d_small, 48)
                b = is_free(pe, ("gz", t))
                nc.tensor.matmul(b[:, 0:256], lrT[:, P * t:P * (t + 1)], wup[:, :],
                                 start=True, stop=True).then_inc(filled(("gz", t)), 1)

            def rowT(c, t):
                src = row if c != C_GQK else grow
                if c == C_GQK:
                    wait_moved(pe, ("proj", c, t))
                else:
                    pe.wait_ge(s["g_rope"], TILES * (1 + (C_AQ, C_AK).index(c)) + t + 1)
                b = is_free(pe, ("rowT", c, t))
                for j in range(4):
                    last = nc.tensor.transpose(b[:, P * j:P * (j + 1)], src[:, t, P * j:P * (j + 1)], ident())
                last.then_inc(filled(("rowT", c, t)), 1)

            def cum(t):
                pe.wait_ge(s["v_lg"], 1)
                pe.wait_ge(d_cst, 16)
                b = is_free(pe, ("cum", t))
                for g in range(2):
                    nc.tensor.matmul(b[:, P * g:P * (g + 1)], lg[:, t, P * g:P * (g + 1)], cst[:, CUM:CUM + P],
                                     start=True, stop=True)
                nc.tensor.matmul(b[:, 256:512], cst[:, REV:REV + P], lg[:, t, :],
                                 start=True, stop=True).then_inc(filled(("cum", t)), 1)

            def pairs(lev, odd):
                key = ("pairs", lev, odd)
                pe.wait_ge(s["v_X"], 2 * (lev + 1))
                b = is_free(pe, key)
                for n in range(GLA_HEADS // 2 * TILES):
                    g, t = divmod(n, TILES)
                    x = X[64 * odd:64 * odd + 64, lev % 2, g, P * t:P * (t + 1)]
                    for part in range(1 if lev == 0 else 2):
                        a, c = (0, 64) if lev == 0 else (64 * part, 64 * part)
                        last = nc.tensor.matmul(b[64 * part:64 * part + 64, 64 * n:64 * (n + 1)],
                                                x[:, a:a + 64], x[:, c:c + 64], start=True, stop=True)
                last.then_inc(filled(key), 1)

            def kv(t):
                if t == TILES - 1:
                    return
                pe.wait_ge(s["g_kt"], t + 1)
                wait_moved(pe, ("proj", C_GV, t))
                b = is_free(pe, ("kv", t))
                for h in range(GLA_HEADS):
                    lo = 64 * (h % 2)
                    last = nc.tensor.matmul(b[lo:lo + 64, P * (h // 2):P * (h // 2 + 1)],
                                            grow[:, t, 256 + 64 * h:256 + 64 * (h + 1)],
                                            gv[:, t, P * h:P * (h + 1)], start=True, stop=True)
                last.then_inc(filled(("kv", t)), 1)

            def glaout(t):
                for lev in (0, LEVELS - 1):
                    for odd in range(2):
                        wait_moved(pe, ("pairs", lev, odd))
                pe.wait_ge(s["v_qi"], 1)
                if t > 0:
                    wait_moved(pe, ("kv", t - 1))
                for odd in range(2):
                    key = ("glaout", t, odd)
                    b = is_free(pe, key)
                    for h in range(odd, GLA_HEADS, 2):
                        lo, o = 64 * odd, b[:, P * (h // 2):P * (h // 2 + 1)]
                        last = nc.tensor.matmul(o, AT[:, h, t, :], gv[:, t, P * h:P * (h + 1)],
                                                start=True, stop=(t == 0))
                        if t > 0:
                            last = nc.tensor.matmul(o, qi[lo:lo + 64, h // 2, P * t:P * (t + 1)],
                                                    S[lo:lo + 64, t - 1, h // 2, :], start=False, stop=True)
                    last.then_inc(filled(key), 1)

            def qk_(t, h):
                n, u, half = (t + 1) * P, unit_no[(t, h)], slice(64 * (h % 2), 64 * (h % 2) + 64)
                if h == 0:
                    wait_moved(pe, ("rowT", C_AK, TILES - 1))
                pe.wait_ge(s["g_ql"], u // 2 + 1)
                b = is_free(pe, ("qk", t, h))
                q_hi, q_lo = (qT_parts[u // 2 % 2][half, part, :] for part in range(2))
                k_hi, k_lo = (a[half, h // 2, 0:n] for a in (kT_hi, kT_lo))
                nc.tensor.matmul(b[:, 0:n], q_hi, k_hi, start=True, stop=False)
                nc.tensor.matmul(b[:, 0:n], q_hi, k_lo, start=False, stop=False)
                nc.tensor.matmul(b[:, 0:n], q_lo, k_hi, start=False, stop=True).then_inc(filled(("qk", t, h)), 1)

            def pT(t, h):
                u = unit_no[(t, h)]
                pe.wait_ge(s["a_p"], u + 1)
                b = is_free(pe, ("pT", t, h))
                for j in range(t + 1):
                    last = nc.tensor.transpose(b[:, P * j:P * (j + 1)], Pb[:, u % 2, P * j:P * (j + 1)], ident())
                last.then_inc(filled(("pT", t, h)), 1)

            def pv(t, h):
                u = unit_no[(t, h)]
                wait_moved(pe, ("pT", t, h))
                if h == 0:
                    wait_moved(pe, ("proj", C_AV, t))
                    is_free(pe, ("att", t))
                b = bank[O_BANK]
                for j in range(t + 1):
                    last = nc.tensor.matmul(b[:, 64 * h:64 * (h + 1)], pTb[:, u % 2, P * j:P * (j + 1)],
                                            av[:, j, 64 * h:64 * (h + 1)], start=(j == 0), stop=(j == t))
                if h == ATT_HEADS - 1:
                    last.then_inc(full[O_BANK], 1)
                else:
                    last.then_inc(s["t_pv"], 1)

            def mixT(t, g):
                pe.wait_ge(s["v_am"], t + 1)
                pe.wait_ge(s["v_gm"], GLA_HEADS * (t + 1))
                b = is_free(pe, ("mixT", t, g))
                for j in range(4):
                    last = nc.tensor.transpose(b[:, P * j:P * (j + 1)], xm[:, t, 4 * g + j::KT], ident())
                last.then_inc(filled(("mixT", t, g)), 1)

            def outp(t, n, half):
                key = ("outp", t, n)
                if t == 0:
                    pe.wait_ge(s["a_wo"], WOUT_PIECES * (half + 1))
                    pe.wait_ge(s["v_wo"], WOUT_PIECES // 2 * (half + 1))
                    pe.wait_ge(s["g_wo"], WOUT_PIECES // 2 * (half + 1))
                wait_moved(pe, ("mixT", t, half))
                b = bank[jobs[key][0]]
                if half == 0:
                    is_free(pe, key)
                for k in range(half * KT // 2, (half + 1) * KT // 2):
                    m_hi, m_lo = mT_hi[t][:, k, :], mT_lo[t][:, k, :]
                    if n == 0:
                        v_hi, v_lo = hT_hi[:, k, :], hT_lo[:, k, :]
                    else:
                        v_hi, v_lo = (a[:, k // 4, k % 4, :] for a in (w_hi, w_lo))
                    nc.tensor.matmul(b[:, :], m_hi, v_hi, start=(k == 0), stop=False)
                    nc.tensor.matmul(b[:, :], m_hi, v_lo, start=False, stop=False)
                    last = nc.tensor.matmul(b[:, :], m_lo, v_hi, start=False, stop=(k == KT - 1))
                if half == 1:
                    last.then_inc(filled(key), 1)

            parts = {"xT": xT, "proj": proj, "idxT": idxT_, "score": score, "gz": gz, "rowT": rowT, "cum": cum,
                     "pairs": pairs, "kv": kv, "glaout": glaout, "qk": qk_, "pT": pT, "pv": pv, "mixT": mixT,
                     "outp": outp}
            for step in plan:
                if step[0] in parts:
                    parts[step[0]](*step[1:])

        @block.scalar
        def _(act):
            act.dma_start(prew[:, :], pre_norm_w.rearrange("(p k) -> p k", k=KT)).then_inc(d_prew, 16)
            act.dma_start(pos[:, :], positions).then_inc(d_pos, 16)
            act.dma_start(wup[:, :], w_up).then_inc(d_small, 16)
            act.dma_start(bgate[:, :], b_gate.partition_broadcast(P)).then_inc(d_small, 16)
            act.dma_start(glaw[:, :], gla_norm_w.partition_broadcast(P)).then_inc(d_small, 16)
            def angles():
                act.wait_ge(s["v_ang"], 9)
                nc.scalar.activation(sind[:, :, 1, :], ang[:, 2, :, :], ACT.Sin).then_inc(s["a_ang"], 1)
                nc.scalar.activation(cosd[:, :, 0, :], ang[:, 3, :, :], ACT.Sin).then_inc(s["a_ang"], 1)
                act.wait_ge(s["a_ang"], 2)
                nc.scalar.activation(sind[:, :, 0, :], sind[:, :, 1, :], ACT.Copy, scale=-1.0).then_inc(s["a_ang"], 1)
                nc.scalar.activation(cosd[:, :, 1, :], cosd[:, :, 0, :], ACT.Copy).then_inc(s["a_ang"], 1)

            def prep(n):
                w = WIDTH[n // 2]
                act.wait_ge(d_raw[n % 2], raw_value(n))
                if n >= 2:
                    half_done(act, n - 2)
                nc.scalar.activation(w_hi[:, n % 2, :, 0:w], raw[:, n % 2, :, 0:w], ACT.Copy).then_inc(s["a_whi"], 1)

            def xT(t, g):
                j = 2 * t + g
                wait_moved(act, ("xT", t, g))
                nc.scalar.activation(hT_hi[:, 4 * g:4 * g + 4, P * t:P * (t + 1)],
                                     row[:, j % 4, :].rearrange("p (k n) -> p k n", k=4),
                                     ACT.Copy).then_inc(s["a_hTh"], 1)

            def ssq_(t):
                act.wait_ge(d_x[t], 16)
                if t > 0:
                    act.wait_ge(s["a_ssq"], t)
                nc.scalar.activation(E[:, :, :].rearrange("p a b -> p (a b)"), xm[:, t, :], ACT.Square,
                                     accum_out=ssq[:, 0, t:t + 1]).then_inc(s["a_ssq"], 1)

            def evac(c, t):
                key = ("proj", c, t)
                b = wait_full(act, key)
                rstd, hrstd = ssq[:, 2, t:t + 1], ssq[:, 3, t:t + 1]
                act.wait_ge(s["g_rstd"], 3)
                if c == C_IDX:
                    nc.scalar.activation(idxrow[:, t, 0:320], b[:, 0:320], ACT.Copy, scale=rstd)
                    nc.scalar.activation(idxrow[:, t, IW0:IW0 + 4], b[:, 320:324], ACT.Copy, scale=rstd)
                    nc.scalar.activation(idxrow[:, t, LR0:LR0 + GATE_RANK], b[:, 324:340], ACT.Copy, scale=rstd)\
                        .then_inc(emptied(key), 1)
                elif c in (C_AGATE, C_GGATE):
                    o = 0 if c == C_AGATE else ATT_W
                    before = t + (TILES if c == C_GGATE else 0)
                    if before > 0:
                        act.wait_ge(s["v_gate"], before)
                    nc.scalar.activation(th[:, :], b[:, :], ACT.Tanh, scale=hrstd)
                    nc.scalar.activation(xm[:, t, o:o + 512], b[:, :], ACT.Copy, scale=hrstd).then_inc(emptied(key), 1)
                else:
                    if c == C_GV and t == 0:
                        for odd in range(2):
                            wait_full(act, ("pairs", LEVELS - 1, odd))
                    dst = {C_AQ: row, C_AK: row, C_GQK: grow, C_AV: av, C_GV: gv}[c]
                    nc.scalar.activation(dst[:, t, :], b[:, :], ACT.Copy, scale=rstd).then_inc(emptied(key), 1)

            def idxT_(t):
                tile = slice(P * t, P * (t + 1))
                b = wait_full(act, ("idxT", t))
                for odd in range(2):
                    half = slice(64 * odd, 64 * odd + 64)
                    nc.scalar.activation(iqT[half, odd::2, tile],
                                         b[half, 0:2 * P].rearrange("p (k n) -> p k n", k=2), ACT.Copy)
                nc.scalar.activation(ikT_hi[:, tile], b[:, 2 * P:3 * P], ACT.Copy)
                nc.scalar.activation(lrT[:, tile], b[0:GATE_RANK, 3 * P:4 * P], ACT.Copy).then_inc(s["a_iT"], 1)

            def score(t, h):
                key, n, i = ("score", t, h), (t + 1) * P, IDX_HEADS * (t - 1) + h
                b = wait_full(act, key)
                if i >= 2:
                    act.wait_ge(s["v_score"], (i - 2) // IDX_HEADS * 5 + (i - 2) % IDX_HEADS + 1)
                nc.scalar.activation(rel[:, i % 2, 0:n], b[:, 0:n], ACT.Relu).then_inc(emptied(key), 1)

            def logalpha():
                for t in range(TILES):
                    wait_moved(act, ("gz", t))
                nc.scalar.activation(lgt[:, :, :], lg[:, :, :], ACT.Abs).then_inc(s["a_la"], 1)
                act.wait_ge(s["a_la"], 1)
                nc.scalar.activation(lgt[:, :, :], lgt[:, :, :], ACT.Exp, scale=-1.0).then_inc(s["a_la"], 1)
                act.wait_ge(s["a_la"], 2)
                nc.scalar.activation(lgt[:, :, :], lgt[:, :, :], ACT.Ln, bias=1.0).then_inc(s["a_la"], 1)

            def cum(t):
                key = ("cum", t)
                b = wait_full(act, key)
                nc.scalar.activation(bT[:, :, P * t:P * (t + 1)], b[:, 0:256].rearrange("p (g n) -> p g n", g=2),
                                     ACT.Copy)
                nc.scalar.activation(lg[:, t, :], b[:, 256:512], ACT.Exp, scale=1 / 16).then_inc(emptied(key), 1)

            def rowT(c, t):
                key = ("rowT", c, t)
                b = wait_full(act, key)[:, :].rearrange("p (k n) -> p k n", k=4)
                if c == C_GQK:
                    nc.scalar.activation(gqkT[:, 0:2, P * t:P * (t + 1)], b[:, 0:2, :], ACT.Copy, scale=GLA_DK ** -0.5)
                    nc.scalar.activation(gqkT[:, 2:4, P * t:P * (t + 1)], b[:, 2:4, :], ACT.Copy)\
                        .then_inc(emptied(key), 1)
                elif c == C_AQ:
                    nc.scalar.activation(aqT[:, :, P * t:P * (t + 1)], b, ACT.Copy).then_inc(emptied(key), 1)
                else:
                    nc.scalar.activation(kT_hi[:, :, P * t:P * (t + 1)], b, ACT.Copy).then_inc(s["a_kh"], 1)

            def decay(lev):
                if lev == LEVELS:
                    return
                half = P // 2 >> lev
                e = E[:, :, :].rearrange("p g (n i) -> p (g n) i", i=2 * half)
                act.wait_ge(s["v_D"], lev + 1)
                nc.scalar.activation(e[:, :, 0:half], e[:, :, 0:half], ACT.Exp, scale=-1 / 16).then_inc(s["a_E"], 1)
                nc.scalar.activation(e[:, :, half:], e[:, :, half:], ACT.Exp, scale=1 / 16).then_inc(s["a_E"], 1)

            def qinter():
                act.wait_ge(s["v_qk"], 3)
                wait_moved(act, ("cum", TILES - 1))
                nc.scalar.activation(E[:, :, :], bT[:, :, :], ACT.Exp, scale=1 / 16).then_inc(s["a_dec"], 1)
                act.wait_ge(s["a_dec"], 1)
                nc.scalar.activation(dec[:, :, :], E[:, :, P - 1::P], ACT.Copy).then_inc(s["a_dec"], 1)
                decay(0)

            def pairs(lev, odd):
                if lev > 0:
                    return
                key = ("pairs", lev, odd)
                b = wait_full(act, key)
                act.wait_ge(s["g_init"], 3)
                nc.scalar.activation(AT[0:64, odd::2, :, 64:128],
                                     b[0:64, :].rearrange("p (g t n) -> p g t n", g=GLA_HEADS // 2, t=TILES),
                                     ACT.Copy).then_inc(emptied(key), 1)

            def qparts(t, h):
                pair = unit_no[(t, h)] // 2
                if h == 0:
                    wait_moved(act, ("rowT", C_AQ, t))
                if pair >= 2:
                    wait_full(act, ("qk", *UNITS[2 * pair - 3]))
                nc.scalar.activation(qT_parts[pair % 2][:, 0, :], aqT[:, h // 2, P * t:P * (t + 1)], ACT.Copy)\
                    .then_inc(s["a_qh"], 1)

            def qk_(t, h):
                u, n = unit_no[(t, h)], (t + 1) * P
                wait_moved(act, ("qk", t, h))
                nc.scalar.activation(Pb[:, u % 2, 0:n], Pb[:, u % 2, 0:n], ACT.Exp, bias=nmax[:, u:u + 1], scale=-1.0,
                                     accum_out=psums[:, u:u + 1]).then_inc(s["a_p"], 1)

            def pT(t, h):
                u, n, key = unit_no[(t, h)], (t + 1) * P, ("pT", t, h)
                if not pT_on_act(u):
                    return
                b = wait_full(act, key)
                if u >= 2:
                    pv_done(act, u - 2)
                nc.scalar.activation(pTb[:, u % 2, 0:n], b[:, 0:n], ACT.Copy).then_inc(emptied(key), 1)

            def glasum(t):
                wait_moved(act, ("glaout", t, 0))
                wait_moved(act, ("glaout", t, 1))
                for h in range(GLA_HEADS):
                    if GLA_HEADS * t + h > 0:
                        act.wait_ge(s["a_gsq"], GLA_HEADS * t + h)
                    nc.scalar.activation(E[:, 0, 0:P], og[:, t % 2, P * h:P * (h + 1)], ACT.Square,
                                         accum_out=gss[:, 0, GLA_HEADS * t + h:GLA_HEADS * t + h + 1])\
                        .then_inc(s["a_gsq"], 1)

            def wprep(j, n):
                act.wait_ge(d_raw[j % 2], raw_value(2 * NC + j))
                if j == 0:
                    half_done(act, 2 * NC - 2)
                if 2 * j == KT // 2:
                    half_done(act, 2 * NC - 1)
                src = raw[:, j % 2, :, :].rearrange("p (k m) n -> p k (m n)", k=2)[:, :, 512 * n:512 * (n + 1)]
                k = 2 * j
                dst = hT_hi[:, k:k + 2, :] if n == 0 else w_hi[:, k // 4, k % 4:k % 4 + 2, :]
                nc.scalar.activation(dst, src, ACT.Copy).then_inc(s["a_wo"], 1)

            def mixT(t, g):
                b = wait_full(act, ("mixT", t, g))
                if t == 1 and g == 0:
                    act.wait_ge(s["a_wo"], 6)
                    act.wait_ge(s["v_wo"], 3)
                    act.wait_ge(s["g_wo"], 3)
                nc.scalar.activation(mT_hi[t][:, 4 * g:4 * g + 4, :], b[:, :].rearrange("p (k n) -> p k n", k=4),
                                     ACT.Copy).then_inc(s["a_mTh"], 1)

            def outp(t, n, half):
                if half == 0:
                    return
                b = wait_full(act, ("outp", t, n))
                if 2 * t + n > 0:
                    act.wait_ge(s["a_osq"], 2 * t + n)
                else:
                    act.wait_ge(s["a_gsq"], GLA_HEADS * TILES)
                nc.scalar.activation(E[:, n, :], b[:, :], ACT.Square, accum_out=oss[:, n, t:t + 1])\
                    .then_inc(s["a_osq"], 1)

            parts = {"prep": prep, "xT": xT, "ssq": ssq_, "angles": angles, "evac": evac, "idxT": idxT_, "score": score,
                     "logalpha": logalpha, "cum": cum, "rowT": rowT, "qinter": qinter, "decay": decay,
                     "pairs": pairs, "qparts": qparts,
                     "qk": qk_,
                     "pT": pT, "glasum": glasum, "wprep": wprep, "mixT": mixT, "outp": outp}
            for step in plan:
                if step[0] in parts:
                    parts[step[0]](*step[1:])

        @block.vector
        def _(dve):
            V = nc.vector

            def angles():
                a, turns, r, c = (ang[:, n, :, :] for n in range(4))
                magic = 1.5 * 2.0 ** 23
                steps = [
                    lambda: V.tensor_tensor(a, pos[:, :].unsqueeze(2).broadcast_to([P, TILES, HALF]),
                                            cst[:, FREQ:FREQ + HALF].unsqueeze(1).broadcast_to([P, TILES, HALF]),
                                            ALU.mult),
                    lambda: V.tensor_scalar(turns, a, 1 / (2 * PI), magic, ALU.mult, ALU.add),
                    lambda: V.tensor_scalar(turns, turns, -magic, None, ALU.add),
                    lambda: V.scalar_tensor_tensor(r, turns, -TWO_PI[0], a, ALU.mult, ALU.add),
                    lambda: V.scalar_tensor_tensor(r, turns, -TWO_PI[1], r, ALU.mult, ALU.add),
                    lambda: V.scalar_tensor_tensor(r, turns, -TWO_PI[2], r, ALU.mult, ALU.add),
                    lambda: V.tensor_scalar(r, r, PI_BELOW, -PI_BELOW, ALU.min, ALU.max),
                    lambda: V.scalar_tensor_tensor(c, r, -1.0, r, ALU.mult, ALU.min),
                    lambda: V.tensor_scalar(c, c, PI / 2, None, ALU.add),
                ]
                dve.wait_ge(d_pos, 16)
                dve.wait_ge(d_cst, 16)
                for n, step in enumerate(steps):
                    if n > 0:
                        dve.wait_ge(s["v_ang"], n)
                    step().then_inc(s["v_ang"], 1)

            def low_h(j):
                dve.wait_ge(s["a_hTh"], j + 1)
                at = (slice(None), slice(KT // 2, KT), slice(P * (j // 2), P * (j // 2 + 1)))
                V.tensor_tensor(hT_lo[at], row[:, j % 4, :].rearrange("p (k n) -> p k n", k=4),
                                hT_hi[at].bitcast(F32), ALU.subtract).then_inc(s["v_hTl"], 1)

            def xT(t, g):
                key, j = ("xT", t, g), 2 * t + g
                b = wait_full(dve, key)
                if j == 0:
                    dve.wait_ge(d_prew, 16)
                if j >= 4:
                    dve.wait_ge(s["g_hTl" if g == 0 else "v_hTl"], (j - 4) // 2 + 1)
                V.tensor_tensor(row[:, j % 4, :].rearrange("p (k n) -> p k n", k=4),
                                b[:, :].rearrange("p (k n) -> p k n", k=4),
                                prew[:, 4 * g:4 * g + 4].unsqueeze(2).broadcast_to([P, 4, P]),
                                ALU.mult).then_inc(emptied(key), 1)
                if g == 1:
                    low_h(j)

            def prep(n):
                if low_on_pool(n):
                    return
                w = WIDTH[n // 2]
                dve.wait_ge(s["a_whi"], n + 1)
                V.tensor_tensor(w_lo[:, n % 2, :, 0:w], raw[:, n % 2, :, 0:w], w_hi[:, n % 2, :, 0:w].bitcast(F32),
                                ALU.subtract).then_inc(s["v_wlo"], 1)

            def evac(c, t):
                if c not in (C_AGATE, C_GGATE):
                    return
                o = 0 if c == C_AGATE else ATT_W
                wait_moved(dve, ("proj", c, t))
                g = xm[:, t, o:o + 512]
                V.scalar_tensor_tensor(g, th[:, :], 1.0, g, ALU.add, ALU.mult).then_inc(s["v_gate"], 1)

            def idxT_(t):
                tile = slice(P * t, P * (t + 1))
                b = wait_full(dve, ("idxT", t))
                dve.wait_ge(s["a_iT"], t + 1)
                for odd in range(2):
                    half, other = (slice(64 * n, 64 * n + 64) for n in (odd, 1 - odd))
                    V.tensor_tensor(iqT[other, odd::2, tile], b[half, 0:2 * P].rearrange("p (k n) -> p k n", k=2),
                                    iqT[half, odd::2, tile].bitcast(F32), ALU.subtract)
                V.tensor_tensor(ikT_lo[:, tile], b[:, 2 * P:3 * P], ikT_hi[:, tile].bitcast(F32), ALU.subtract)\
                    .then_inc(emptied(("idxT", t)), 1)

            def cand(t):
                at = sum((u + 1) * P for u in range(1, t))
                return work[:, at:at + (t + 1) * P]

            def bias_of(t):
                if t == 0:
                    return cst[:, CAUSAL:CAUSAL + P]
                at = sum((u + 1) * P for u in range(1, t))
                return bias[:, at:at + (t + 1) * P]

            def score(t, h):
                n, i = (t + 1) * P, IDX_HEADS * (t - 1) + h
                wait_moved(dve, ("score", t, h))
                dst, wt = cand(t), iw[:, t, h:h + 1]
                if h == 0:
                    V.tensor_scalar(dst, rel[:, i % 2, 0:n], wt, None, ALU.mult).then_inc(s["v_score"], 1)
                    return
                dve.wait_ge(s["v_score"], 5 * (t - 1) + h)
                V.scalar_tensor_tensor(dst, rel[:, i % 2, 0:n], wt, dst, ALU.mult, ALU.add).then_inc(s["v_score"], 1)
                if h == IDX_HEADS - 1:
                    dve.wait_ge(s["v_score"], 5 * (t - 1) + h + 1)
                    dst = dst[:, t * P:(t + 1) * P]
                    V.tensor_tensor(dst, dst, cst[:, CAUSAL:CAUSAL + P], ALU.add).then_inc(s["v_score"], 1)

            def topk(t, r):
                m = ROUNDS * (t - 1) + r
                if r == 0:
                    dve.wait_ge(s["v_score"], 5 * t)
                if m > 0:
                    dve.wait_ge(s["v_cand"], m)
                V.max(best[:, :], cand(t)).then_inc(s["v_best"], 1)
                dve.wait_ge(s["v_best"], m + 1)
                V.match_replace(cand(t), best[:, :], cand(t), TAKEN).then_inc(s["v_cand"], 1)
                if r == ROUNDS - 1:
                    dve.wait_ge(s["v_cand"], m + 1)
                    V.tensor_scalar(bias_of(t), cand(t), TAKEN, NEG, ALU.is_gt, ALU.mult).then_inc(s["v_bias"], 1)

            def gz(t):
                key = ("gz", t)
                b = wait_full(dve, key)
                if t == 0:
                    dve.wait_ge(d_small, 48)
                V.tensor_tensor(lg[:, t, :], b[:, 0:256], bgate[:, :], ALU.add).then_inc(emptied(key), 1)

            def logalpha():
                dve.wait_ge(s["a_la"], 3)
                V.scalar_tensor_tensor(lg[:, :, :], lg[:, :, :], 0.0, lgt[:, :, :], ALU.min, ALU.subtract)\
                    .then_inc(s["v_lg"], 1)

            def qkdiag():
                for t in range(TILES):
                    wait_moved(dve, ("proj", C_GQK, t))
                prod = E[:, :, :].rearrange("p g (t n) -> p (g t) n", n=256)
                V.tensor_tensor(prod, grow[:, :, 0:256], grow[:, :, 256:512], ALU.mult).then_inc(s["v_qk"], 1)
                dve.wait_ge(s["v_qk"], 1)
                V.tensor_reduce(qkd[:, 0, :], E[:, :, :].rearrange("p g (n d) -> p (g n) d", d=GLA_DK), AX.X,
                                ALU.add).then_inc(s["v_qk"], 1)
                dve.wait_ge(s["v_qk"], 2)
                V.tensor_scalar(qkd[:, 1, :], qkd[:, 0, :], GLA_DK ** -0.5, None, ALU.mult).then_inc(s["v_qk"], 1)

            def rowT(c, t):
                if c != C_AK:
                    return
                at = (slice(None), slice(None), slice(P * t, P * (t + 1)))
                b = wait_full(dve, ("rowT", c, t))[:, :].rearrange("p (k n) -> p k n", k=4)
                dve.wait_ge(s["a_kh"], t + 1)
                V.tensor_tensor(kT_lo[at], b, kT_hi[at].bitcast(F32), ALU.subtract)\
                    .then_inc(emptied(("rowT", c, t)), 1)

            def blocks(a, half):
                return a.rearrange("p g (n i) -> p (g n) i", i=2 * half)

            def diff(lev):
                half = P // 2 >> lev
                b, e = blocks(bT[:, :, :], half), blocks(E[:, :, :], half)
                n = 2 * SEQ // (2 * half)
                if lev == 0:
                    dve.wait_ge(s["v_qi"], 1)
                else:
                    dve.wait_ge(s["v_X"], 2 * lev)
                V.tensor_tensor(e, b, b[:, :, half - 1:half].broadcast_to([P, n, 2 * half]), ALU.subtract)\
                    .then_inc(s["v_D"], 1)

            def qinter():
                wait_moved(dve, ("rowT", C_GQK, TILES - 1))
                dve.wait_ge(s["a_dec"], 2)
                V.tensor_tensor(qi[:, :, :], gqkT[:, 0:2, :], E[:, :, :], ALU.mult).then_inc(s["v_qi"], 1)
                diff(0)

            def level(lev):
                half = P // 2 >> lev
                e, x = blocks(E[:, :, :], half), blocks(X[:, lev % 2, :, :], half)
                q, k = blocks(gqkT[:, 0:2, :], half), blocks(gqkT[:, 2:4, :], half)
                if lev >= 2:
                    for odd in range(2):
                        wait_full(dve, ("pairs", lev - 2, odd))
                dve.wait_ge(s["a_E"], 2 * (lev + 1))
                V.tensor_tensor(x[:, :, 0:half], k[:, :, 0:half], e[:, :, 0:half], ALU.mult).then_inc(s["v_X"], 1)
                V.tensor_tensor(x[:, :, half:], q[:, :, half:], e[:, :, half:], ALU.mult).then_inc(s["v_X"], 1)
                if lev + 1 < LEVELS:
                    diff(lev + 1)

            def pairs(lev, odd):
                if lev == 0:
                    return
                key = ("pairs", lev, odd)
                b = wait_full(dve, key)
                if lev == 1:
                    dve.wait_ge(s["g_init"], 3)
                for part in range(2):
                    at = slice(64 * part, 64 * part + 64)
                    last = V.copy_predicated(
                        AT[at, odd::2, :, at],
                        lvl[at, lev, at].unsqueeze(1).unsqueeze(1).broadcast_to([64, GLA_HEADS // 2, TILES, 64]),
                        b[at, :].rearrange("p (g t n) -> p g t n", g=GLA_HEADS // 2, t=TILES))
                last.then_inc(emptied(key), 1)

            def kv(t):
                if t == TILES - 1:
                    return
                key = ("kv", t)
                b = wait_full(dve, key)
                if t == 0:
                    V.tensor_copy(S[:, 0, :, :], b[:, 0:256].rearrange("p (g n) -> p g n", g=2))\
                        .then_inc(emptied(key), 1)
                    return
                wait_moved(dve, ("kv", t - 1))
                dve.wait_ge(s["a_dec"], 2)
                for g in range(2):
                    last = V.scalar_tensor_tensor(S[:, t, g, :], S[:, t - 1, g, :], dec[:, g, t:t + 1],
                                                  b[:, P * g:P * (g + 1)], ALU.mult, ALU.add)
                last.then_inc(emptied(key), 1)

            def glaout(t):
                dve.wait_ge(s["g_kt"], TILES - 1)
                if t >= 2:
                    dve.wait_ge(s["v_gm"], GLA_HEADS * (t - 1))
                for odd in range(2):
                    key = ("glaout", t, odd)
                    b = wait_full(dve, key)
                    for h in range(odd, GLA_HEADS, 2):
                        n = GLA_HEADS * t + h
                        last = V.scalar_tensor_tensor(og[:, t % 2, P * h:P * (h + 1)], gv[:, t, P * h:P * (h + 1)],
                                                      qkd[:, 1, n:n + 1], b[:, P * (h // 2):P * (h // 2 + 1)],
                                                      ALU.mult, ALU.add)
                    last.then_inc(emptied(key), 1)

            def glafin(t):
                dve.wait_ge(s["g_grs"], 2 * (t + 1))
                dve.wait_ge(s["g_gate"], t + 1)
                for h in range(GLA_HEADS):
                    n = GLA_HEADS * t + h
                    g = xm[:, t, ATT_W + P * h:ATT_W + P * (h + 1)]
                    V.scalar_tensor_tensor(g, og[:, t % 2, P * h:P * (h + 1)], gss[:, 2, n:n + 1], g, ALU.mult, ALU.mult)\
                        .then_inc(s["v_gm"], 1)

            def qk_(t, h):
                u, n, key = unit_no[(t, h)], (t + 1) * P, ("qk", t, h)
                b = wait_full(dve, key)
                if u >= 2:
                    wait_full(dve, ("pT", *UNITS[u - 2]))
                if h == 0 and t > 0:
                    dve.wait_ge(s["v_bias"], t)
                V.tensor_tensor_reduce(Pb[:, u % 2, 0:n], b[:, 0:n], bias_of(t), -ATT_HD ** -0.5, 3e38,
                                       ALU.add, ALU.min, nmax[:, u:u + 1]).then_inc(emptied(key), 1)

            def pT(t, h):
                u, n, key = unit_no[(t, h)], (t + 1) * P, ("pT", t, h)
                if pT_on_act(u):
                    return
                b = wait_full(dve, key)
                if u >= 2:
                    pv_done(dve, u - 2)
                V.tensor_copy(pTb[:, u % 2, 0:n], b[:, 0:n]).then_inc(emptied(key), 1)

            def attfin(t):
                key = ("att", t)
                dve.wait_ge(s["a_p"], ATT_HEADS * (t + 1))
                V.reciprocal(rinv[:, ATT_HEADS * t:ATT_HEADS * (t + 1)], psums[:, ATT_HEADS * t:ATT_HEADS * (t + 1)])\
                    .then_inc(s["v_rinv"], 1)
                b = wait_full(dve, key)
                dve.wait_ge(s["v_gate"], t + 1)
                V.tensor_tensor(xm[:, t, 0:ATT_W], b[:, :], xm[:, t, 0:ATT_W], ALU.mult).then_inc(emptied(key), 1)
                wait_moved(dve, key)
                dve.wait_ge(s["v_rinv"], t + 1)
                heads = xm[:, t, 0:ATT_W].rearrange("p (h n) -> p h n", h=ATT_HEADS)
                V.tensor_tensor(heads, heads, rinv[:, ATT_HEADS * t:ATT_HEADS * (t + 1)].unsqueeze(2)
                                .broadcast_to([P, ATT_HEADS, ATT_HD]), ALU.mult).then_inc(s["v_am"], 1)

            def wprep(j, n):
                if n == 1:
                    return
                src = raw[:, j % 2, :, :].rearrange("p (k m) n -> p k (m n)", k=2)[:, :, 0:512]
                k = 2 * j
                dve.wait_ge(s["a_wo"], 2 * j + 1)
                V.tensor_tensor(hT_lo[:, k:k + 2, :], src, hT_hi[:, k:k + 2, :].bitcast(F32), ALU.subtract)\
                    .then_inc(s["v_wo"], 1)

            def mixT(t, g):
                key = ("mixT", t, g)
                dve.wait_ge(s["a_mTh"], 2 * t + g + 1)
                b = bank[jobs[key][0]]
                V.tensor_tensor(mT_lo[t][:, 4 * g:4 * g + 4, :], b[:, :].rearrange("p (k n) -> p k n", k=4),
                                mT_hi[t][:, 4 * g:4 * g + 4, :].bitcast(F32), ALU.subtract)\
                    .then_inc(emptied(key), 1)

            def weighted(t, n):
                key = ("outp", t, n)
                b = wait_full(dve, key)
                dve.wait_ge(s["a_osq"], 2 * t + n + 1)
                cols = slice(512 * n, 512 * (n + 1))
                V.tensor_tensor(yout[:, t % 2, cols], b[:, :], postw[:, cols], ALU.mult).then_inc(emptied(key), 1)

            def outp(t, n, half):
                if n > 0 or half == 0:
                    return
                if t == 0:
                    dve.wait_ge(d_post, 16)
                if t >= 2:
                    dve.wait_ge(d_out[t % 2], 32 * (t // 2))
                weighted(t, 0)

            def fin(t):
                c = slice(t, t + 1)
                dve.wait_ge(s["a_osq"], 2 * (t + 1))
                dve.wait_ge(s["g_ors"], 2 * t + 1)
                V.scalar_tensor_tensor(oss[:, 3, c], oss[:, 1, c], 1 / D_MODEL, oss[:, 2, c], ALU.mult, ALU.add)\
                    .then_inc(s["v_mean"], 1)
                weighted(t, 1)
                dve.wait_ge(s["g_ors"], 2 * t + 2)
                dve.wait_ge(d_xre[t % 2], 16 * (t // 2 + 1))
                for n in range(2):
                    wait_moved(dve, ("outp", t, n))
                    y = yout[:, t % 2, 512 * n:512 * (n + 1)]
                    V.scalar_tensor_tensor(y, y, oss[:, 4, c], xre[:, t % 2, 512 * n:512 * (n + 1)],
                                           ALU.mult, ALU.add).then_inc(s["v_y"], 1)

            parts = {"prep": prep, "xT": xT, "angles": angles, "evac": evac, "idxT": idxT_, "rowT": rowT, "score": score,
                     "topk": topk, "gz": gz,
                     "logalpha": logalpha, "qkdiag": qkdiag, "qinter": qinter, "level": level, "pairs": pairs,
                     "kv": kv, "glaout": glaout, "glafin": glafin, "qk": qk_, "pT": pT, "attfin": attfin,
                     "wprep": wprep, "mixT": mixT, "outp": outp, "fin": fin}
            for step in plan:
                if step[0] in parts:
                    parts[step[0]](*step[1:])

        @block.gpsimd
        def _(pool):
            G = nc.gpsimd
            G.memset(pwr[:, :], -0.5).then_inc(s["g_init"], 1)
            roped = [0]

            def masks():
                pool.wait_ge(d_mask, 16)
                G.tensor_copy(lvl[:, :, :], lvl_in[:, :, :]).then_inc(s["g_init"], 1)
                pool.wait_ge(s["g_init"], 2)
                G.memset(AT[:, :, :, :], 0.0).then_inc(s["g_init"], 1)

            def xT(t, g):
                if g == 1:
                    return
                j = 2 * t
                pool.wait_ge(s["a_hTh"], j + 1)
                at = (slice(None), slice(4 * g, 4 * g + 4), slice(P * t, P * (t + 1)))
                G.tensor_tensor(hT_lo[at], row[:, j % 4, :].rearrange("p (k n) -> p k n", k=4),
                                hT_hi[at].bitcast(F32), ALU.subtract).then_inc(s["g_hTl"], 1)

            def prep(n):
                if not low_on_pool(n):
                    return
                w = WIDTH[n // 2]
                pool.wait_ge(s["a_whi"], n + 1)
                G.tensor_tensor(w_lo[:, n % 2, :, 0:w], raw[:, n % 2, :, 0:w], w_hi[:, n % 2, :, 0:w].bitcast(F32),
                                ALU.subtract).then_inc(s["g_wlo"], 1)

            def wprep(j, n):
                if n == 0:
                    return
                src = raw[:, j % 2, :, :].rearrange("p (k m) n -> p k (m n)", k=2)[:, :, 512:1024]
                at = (slice(None), j // 2, slice(2 * j % 4, 2 * j % 4 + 2))
                pool.wait_ge(s["a_wo"], 2 * j + 2)
                G.tensor_tensor(w_lo[at], src, w_hi[at].bitcast(F32), ALU.subtract).then_inc(s["g_wo"], 1)

            def ssq_(t):
                if t < TILES - 1:
                    return
                pool.wait_ge(s["g_init"], 1)
                pool.wait_ge(s["a_ssq"], TILES)
                G.tensor_scalar(ssq[:, 1, :], ssq[:, 0, :], 1 / D_MODEL, EPS, ALU.mult, ALU.add)\
                    .then_inc(s["g_rstd"], 1)
                pool.wait_ge(s["g_rstd"], 1)
                G.tensor_tensor(ssq[:, 2, :], ssq[:, 1, :], pwr[:, :].broadcast_to([P, TILES]), ALU.pow)\
                    .then_inc(s["g_rstd"], 1)
                pool.wait_ge(s["g_rstd"], 2)
                G.tensor_scalar(ssq[:, 3, :], ssq[:, 2, :], 0.5, None, ALU.mult).then_inc(s["g_rstd"], 1)

            def rope(a, t):
                heads = a.shape[1]
                x4 = a[:, :, 0:2 * HALF]
                by_cos, by_sin = (ropet[:, n, 0:heads, :] for n in range(2))
                over = [P, heads, HALF]
                if roped[0] > 0:
                    pool.wait_ge(s["g_rope"], roped[0])
                else:
                    pool.wait_ge(s["a_ang"], 4)
                roped[0] += 1
                G.tensor_tensor(by_cos, x4, cosd[:, t, :, :].rearrange("p a b -> p (a b)").unsqueeze(1)
                                .broadcast_to([P, heads, 2 * HALF]), ALU.mult).then_inc(s["g_ropet"], 1)
                for n in range(2):
                    G.tensor_tensor(by_sin[:, :, HALF * n:HALF * (n + 1)], x4[:, :, HALF * (1 - n):HALF * (2 - n)],
                                    sind[:, t, n, :].unsqueeze(1).broadcast_to(over), ALU.mult)\
                        .then_inc(s["g_ropet"], 1)
                pool.wait_ge(s["g_ropet"], 3 * roped[0])
                return G.tensor_tensor(x4, by_cos, by_sin, ALU.add)

            def evac(c, t):
                if c == C_IDX:
                    wait_moved(pool, ("proj", c, t))
                    rope(idxrow[:, t, 0:320].rearrange("p (h n) -> p h n", h=5), t).then_inc(s["g_iw"], 1)
                    G.tensor_scalar(iw[:, t, :], idxrow[:, t, IW0:IW0 + IDX_HEADS], (IDX_HEADS * IDX_HD) ** -0.5, None,
                                    ALU.mult).then_inc(s["g_iw"], 1)
                    pool.wait_ge(s["g_iw"], 2 * (t + 1))
                    G.tensor_copy(idxrow[:, t, 320:384], idxrow[:, t, 256:320]).then_inc(s["g_rope"], 1)
                elif c in (C_AQ, C_AK):
                    wait_moved(pool, ("proj", c, t))
                    rope(row[:, t, :].rearrange("p (h n) -> p h n", h=ATT_HEADS), t).then_inc(s["g_rope"], 1)
                elif c == C_GGATE:
                    pool.wait_ge(s["v_gate"], TILES + t + 1)
                    if t == 0:
                        pool.wait_ge(d_small, 48)
                    g = xm[:, t, ATT_W:].rearrange("p (h n) -> p h n", h=GLA_HEADS)
                    G.tensor_tensor(g, g, glaw[:, :].unsqueeze(1).broadcast_to([P, GLA_HEADS, GLA_DV]), ALU.mult)\
                        .then_inc(s["g_gate"], 1)

            def level(lev):
                if lev > 0:
                    return
                pool.wait_ge(s["v_qk"], 3)
                for t in range(TILES - 1):
                    wait_moved(pool, ("rowT", C_GQK, t))
                    wait_moved(pool, ("cum", t))
                    k = grow[:, t, 256:512]
                    G.tensor_tensor(k, k, lg[:, t, :], ALU.mult).then_inc(s["g_kt"], 1)

            def qparts(t, h):
                pair = unit_no[(t, h)] // 2
                pool.wait_ge(s["a_qh"], pair + 1)
                parts = qT_parts[pair % 2]
                G.tensor_tensor(parts[:, 1, :], aqT[:, h // 2, P * t:P * (t + 1)], parts[:, 0, :].bitcast(F32),
                                ALU.subtract).then_inc(s["g_ql"], 1)

            def glasum(t):
                n = GLA_HEADS * t
                pool.wait_ge(s["a_gsq"], n + GLA_HEADS)
                G.tensor_scalar(gss[:, 1, n:n + 4], gss[:, 0, n:n + 4], 1 / GLA_DV, EPS, ALU.mult, ALU.add)\
                    .then_inc(s["g_grs"], 1)
                pool.wait_ge(s["g_grs"], 2 * t + 1)
                G.tensor_tensor(gss[:, 2, n:n + 4], gss[:, 1, n:n + 4], pwr[:, :].broadcast_to([P, 4]), ALU.pow)\
                    .then_inc(s["g_grs"], 1)

            def outp(t, n, half):
                if n > 0 or half == 0:
                    return
                pool.wait_ge(s["a_osq"], 2 * t + 1)
                c = slice(t, t + 1)
                G.tensor_scalar(oss[:, 2, c], oss[:, 0, c], 1 / D_MODEL, EPS, ALU.mult, ALU.add)\
                    .then_inc(s["g_ors"], 1)

            def fin(t):
                c = slice(t, t + 1)
                pool.wait_ge(s["v_mean"], t + 1)
                G.tensor_tensor(oss[:, 4, c], oss[:, 3, c], pwr[:, :], ALU.pow).then_inc(s["g_ors"], 1)

            parts = {"masks": masks, "xT": xT, "prep": prep, "wprep": wprep, "ssq": ssq_, "evac": evac, "level": level,
                     "qparts": qparts,
                     "glasum": glasum, "outp": outp, "fin": fin}
            for step in plan:
                if step[0] in parts:
                    parts[step[0]](*step[1:])


def kernel(**inputs):
    import numpy as np
    import concourse.bacc as bacc
    from concourse.bass_utils import run_bass_kernel_spmd as run

    nc = bacc.Bacc("TRN2", target_bir_lowering=False, num_devices=1)
    i = np.arange(P)
    consts = np.zeros((P, NCONST), np.float32)
    consts[:, IDENT:IDENT + P] = np.eye(P)
    consts[:, CUM:CUM + P] = i[:, None] <= i[None, :]
    consts[:, REV:REV + P] = i[:, None] > i[None, :]
    consts[:, CAUSAL:CAUSAL + P] = np.where(i[None, :] <= i[:, None], 0.0, NEG)
    freq = np.float32(500000.0) ** (-np.arange(0, 2 * HALF, 2, dtype=np.float32) / np.float32(2 * HALF))
    consts[:, FREQ:FREQ + HALF] = freq
    far = i[:, None] ^ i[None, :]
    masks = np.stack([(far >> (LEVELS - 1 - lev) == 1) & (i[None, :] > i[:, None]) for lev in range(LEVELS)], 1)
    arrays, aps = {}, []
    for name in ("x", "positions", "w_in", "w_gla_gate_up", "b_gla_gate", "gla_norm_w", "w_out", "pre_norm_w",
                 "post_norm_w"):
        arrays["in_" + name] = np.ascontiguousarray(inputs[name])
    arrays["in_positions"] = np.ascontiguousarray(arrays["in_positions"].reshape(TILES, P).T)
    arrays["in_consts"] = consts
    arrays["in_masks"] = masks.astype(np.int32)
    for name, a in arrays.items():
        aps.append(nc.dram_tensor(name, a.shape, mybir.dt.from_np(a.dtype), kind="ExternalInput").ap())
    out = nc.dram_tensor("out", (1, SEQ, D_MODEL), F32, kind="ExternalOutput").ap()
    layer_kernel(nc, *aps, out)
    return run(nc, [arrays], core_ids=[0]).results[0]["out"]
```
